# Optimizing a Trainium2 kernel written in Bass

```python
import math
import jax, jax.numpy as jnp
from jax import lax
import numpy as np

'''Hybrid decoder trunk, DEPTH layers, causal everywhere.
Even layers: pre-RMSNorm -> ONE combined input projection whose columns are split between
  (A) multi-scale retention heads (chunkwise recurrent form, RetNet) and
  (B) dilated sliding-window attention heads (LongNet mixture of (window, dilation) patterns),
  outputs concatenated -> ONE output projection -> residual.
Odd layers: pre-RMSNorm -> (C) sliding-window GQA with learned attention sinks -> residual.
Every layer: pre-RMSNorm -> squared-ReLU MLP -> residual.
Inputs: x (BATCH, SEQ, D_MODEL) float32, positions (BATCH, SEQ) int32, per-layer weights.
Output: (BATCH, SEQ, D_MODEL).
'''

D_MODEL = 1024
BATCH = 1
SEQ = 1024
DEPTH = 2

HEAD_DIM = 64
BLOCK = 128
EPS = 1e-6
RET_HEADS = 4
RET_QK_DIM = 64
RET_V_DIM = 128
RET_CHUNK = 128
RET_THETA = 10000.0
DIL_HEADS = 8
DIL_PATTERNS = ((128, 1), (512, 4), (2048, 16))
SWA_Q_HEADS = 16
SWA_KV_HEADS = 4
SWA_WINDOW = 128
ROPE_THETA = 500000.0
ROPE_DIMS = HEAD_DIM // 4
D_FF = 4 * D_MODEL
EVEN_SPLITS = (RET_HEADS * RET_QK_DIM, RET_HEADS * RET_QK_DIM, RET_HEADS * RET_V_DIM, RET_HEADS * RET_V_DIM,
               DIL_HEADS * HEAD_DIM, DIL_HEADS * HEAD_DIM, DIL_HEADS * HEAD_DIM)
EVEN_IN = sum(EVEN_SPLITS)
EVEN_MIX = RET_HEADS * RET_V_DIM + DIL_HEADS * HEAD_DIM
SWA_SPLITS = (SWA_Q_HEADS * HEAD_DIM, SWA_KV_HEADS * HEAD_DIM, SWA_KV_HEADS * HEAD_DIM)
SWA_IN = sum(SWA_SPLITS)
SWA_MIX = SWA_Q_HEADS * HEAD_DIM

kernel_name = 'hybrid_retention_dilated_swa_block'

def rmsnorm(x, g):
    xf = x.astype(jnp.float32)
    y = xf * lax.rsqrt(jnp.mean(xf * xf, axis=-1, keepdims=True) + EPS)
    return (y * g.astype(jnp.float32)).astype(x.dtype)

def to_heads(t, n_heads):
    b, s, _ = t.shape
    return t.reshape(b, s, n_heads, -1).transpose(0, 2, 1, 3)

def from_heads(t):
    b, h, s, d = t.shape
    return t.transpose(0, 2, 1, 3).reshape(b, s, h * d)

def rope(x, pos, n_rot, theta):
    half = n_rot // 2
    inv = jnp.power(jnp.float32(theta), -jnp.arange(half, dtype=jnp.float32) * (2.0 / n_rot))
    ang = pos.astype(jnp.float32)[:, None, :, None] * inv
    cos, sin = jnp.cos(ang), jnp.sin(ang)
    xf = x.astype(jnp.float32)
    x1, x2, rest = xf[..., :half], xf[..., half:n_rot], xf[..., n_rot:]
    return jnp.concatenate([x1 * cos - x2 * sin, x2 * cos + x1 * sin, rest], axis=-1)

def banded_attn(q, k, v, max_dist, sinks=None):
    b, hk, g, L, d = q.shape
    bs = math.gcd(L, BLOCK)
    nb = L // bs
    P = max_dist
    kp = jnp.pad(k.astype(jnp.float32), ((0, 0), (0, 0), (P, 0), (0, 0)))
    vp = jnp.pad(v.astype(jnp.float32), ((0, 0), (0, 0), (P, 0), (0, 0)))
    idx = (jnp.arange(nb) * bs)[:, None] + jnp.arange(bs + P)[None, :]
    kb = kp[:, :, idx]
    vb = vp[:, :, idx]
    qb = q.astype(jnp.float32).reshape(b, hk, g, nb, bs, d)
    s = jnp.einsum('bhgnqd,bhnkd->bhgnqk', qb, kb) * (d ** -0.5)
    qpos = jnp.arange(L).reshape(nb, bs)
    kpos = idx - P
    dist = qpos[:, :, None] - kpos[:, None, :]
    valid = (dist >= 0) & (dist <= max_dist) & (kpos[:, None, :] >= 0)
    s = jnp.where(valid, s, -jnp.inf)
    m = jnp.max(s, axis=-1, keepdims=True)
    if sinks is not None:
        sk = sinks.astype(jnp.float32).reshape(1, hk, g, 1, 1, 1)
        m = jnp.maximum(m, sk)
    p = jnp.exp(s - m)
    den = jnp.sum(p, axis=-1, keepdims=True)
    if sinks is not None:
        den = den + jnp.exp(sk - m)
    o = jnp.einsum('bhgnqk,bhnkd->bhgnqd', p, vb) / den
    lse = (m + jnp.log(den))[..., 0]
    return o.reshape(b, hk, g, L, d), lse.reshape(b, hk, g, L)

def dilated_attention(q, k, v):
    b, h, S, d = q.shape
    outs, lses = [], []
    for w, r in DIL_PATTERNS:
        L = S // r
        def split(t):
            return t.reshape(b, h, L, r, d).transpose(0, 1, 3, 2, 4).reshape(b, h * r, L, d)
        o, lse = banded_attn(split(q)[:, :, None], split(k), split(v), w // r)
        outs.append(o[:, :, 0].reshape(b, h, r, L, d).transpose(0, 1, 3, 2, 4).reshape(b, h, S, d))
        lses.append(lse[:, :, 0].reshape(b, h, r, L).transpose(0, 1, 3, 2).reshape(b, h, S))
    wts = jax.nn.softmax(jnp.stack(lses, axis=0), axis=0)
    return jnp.sum(wts[..., None] * jnp.stack(outs, axis=0), axis=0)

def retention(q, k, v):
    b, h, S, dk = q.shape
    dv = v.shape[-1]
    C = math.gcd(S, RET_CHUNK)
    nc = S // C
    log_gamma = jnp.log1p(-jnp.exp2(-5.0 - jnp.arange(h, dtype=jnp.float32)))
    qc = q.reshape(b, h, nc, C, dk)
    kc = k.reshape(b, h, nc, C, dk)
    vc = v.astype(jnp.float32).reshape(b, h, nc, C, dv)
    i = jnp.arange(C, dtype=jnp.float32)
    diff = i[:, None] - i[None, :]
    decay = jnp.where(diff >= 0, jnp.exp(log_gamma[:, None, None] * jnp.maximum(diff, 0.0)), 0.0)
    scores = jnp.einsum('bhncd,bhnkd->bhnck', qc, kc) * decay[None, :, None]
    o_inner = jnp.einsum('bhnck,bhnkv->bhncv', scores, vc)
    xi = jnp.exp(log_gamma[:, None] * (i + 1.0))
    zeta = jnp.exp(log_gamma[:, None] * (C - 1.0 - i))
    chunk_decay = jnp.exp(log_gamma * C)
    kz = kc * zeta[None, :, None, :, None]

    def step(R, inp):
        q_n, kz_n, v_n = inp
        o = jnp.einsum('bhcd,bhdv->bhcv', q_n, R)
        R = R * chunk_decay[None, :, None, None] + jnp.einsum('bhcd,bhcv->bhdv', kz_n, v_n)
        return R, o

    R0 = jnp.zeros((b, h, dk, dv), jnp.float32)
    _, o_cross = lax.scan(step, R0, (qc.transpose(2, 0, 1, 3, 4), kz.transpose(2, 0, 1, 3, 4),
                                     vc.transpose(2, 0, 1, 3, 4)))
    o_cross = o_cross.transpose(1, 2, 0, 3, 4) * xi[None, :, None, :, None]
    return (o_inner + o_cross).reshape(b, h, S, dv)

def even_mixer(h, positions, w_in, w_out, gn_gain, q_gain, k_gain):
    proj = h @ w_in
    cuts = [int(c) for c in np.cumsum(EVEN_SPLITS)[:-1]]
    rq, rk, rv, rg, dq, dk, dv = jnp.split(proj, cuts, axis=-1)
    rq = rope(to_heads(rq, RET_HEADS), positions, RET_QK_DIM, RET_THETA)
    rk = rope(to_heads(rk, RET_HEADS), positions, RET_QK_DIM, RET_THETA) * (RET_QK_DIM ** -0.5)
    ro = retention(rq, rk, to_heads(rv, RET_HEADS))
    mu = jnp.mean(ro, axis=-1, keepdims=True)
    var = jnp.mean(jnp.square(ro - mu), axis=-1, keepdims=True)
    ro = (ro - mu) * lax.rsqrt(var + EPS) * gn_gain.astype(jnp.float32)[None, :, None, :]
    ra = jax.nn.silu(rg.astype(jnp.float32)) * from_heads(ro)
    dq = rope(rmsnorm(to_heads(dq, DIL_HEADS), q_gain), positions, ROPE_DIMS, ROPE_THETA)
    dk = rope(rmsnorm(to_heads(dk, DIL_HEADS), k_gain), positions, ROPE_DIMS, ROPE_THETA)
    da = from_heads(dilated_attention(dq, dk, to_heads(dv, DIL_HEADS).astype(jnp.float32)))
    mixed = jnp.concatenate([ra, da], axis=-1).astype(h.dtype)
    return mixed @ w_out

def swa_mixer(h, positions, w_qkv, b_qkv, w_out, q_gain, k_gain, sinks):
    b, S, _ = h.shape
    g = SWA_Q_HEADS // SWA_KV_HEADS
    proj = h @ w_qkv + b_qkv
    cuts = [int(c) for c in np.cumsum(SWA_SPLITS)[:-1]]
    q, k, v = jnp.split(proj, cuts, axis=-1)
    q = rope(rmsnorm(to_heads(q, SWA_Q_HEADS), q_gain), positions, ROPE_DIMS, ROPE_THETA)
    k = rope(rmsnorm(to_heads(k, SWA_KV_HEADS), k_gain), positions, ROPE_DIMS, ROPE_THETA)
    v = to_heads(v, SWA_KV_HEADS)
    q = q.reshape(b, SWA_KV_HEADS, g, S, HEAD_DIM)
    o, _ = banded_attn(q, k, v, SWA_WINDOW - 1, sinks.reshape(SWA_KV_HEADS, g))
    o = o.reshape(b, SWA_Q_HEADS, S, HEAD_DIM)
    return from_heads(o).astype(h.dtype) @ w_out

def sq_relu_mlp(h, w_up, w_down):
    return jnp.square(jax.nn.relu(h @ w_up)) @ w_down

def setup_inputs(seed: int = 0) -> dict:
    key = jax.random.key(seed)
    ks = jax.random.split(key, 20)
    ne, no = (DEPTH + 1) // 2, DEPTH // 2
    f32 = jnp.float32

    def w(k, shape, fan_in):
        return jax.random.normal(k, shape, f32) * (fan_in ** -0.5)

    def gain(k, shape):
        return 1.0 + 0.05 * jax.random.normal(k, shape, f32)

    return {
        'x': jax.random.normal(ks[0], (BATCH, SEQ, D_MODEL), f32),
        'positions': jnp.broadcast_to(jnp.arange(SEQ, dtype=jnp.int32), (BATCH, SEQ)),
        'norm_mix': gain(ks[1], (DEPTH, D_MODEL)),
        'norm_mlp': gain(ks[2], (DEPTH, D_MODEL)),
        'mlp_w_up': w(ks[3], (DEPTH, D_MODEL, D_FF), D_MODEL),
        'mlp_w_down': w(ks[4], (DEPTH, D_FF, D_MODEL), D_FF),
        'hyb_w_in': w(ks[5], (ne, D_MODEL, EVEN_IN), D_MODEL),
        'hyb_w_out': w(ks[6], (ne, EVEN_MIX, D_MODEL), EVEN_MIX),
        'ret_gn_gain': gain(ks[7], (ne, RET_HEADS, RET_V_DIM)),
        'dil_q_gain': gain(ks[8], (ne, HEAD_DIM)),
        'dil_k_gain': gain(ks[9], (ne, HEAD_DIM)),
        'swa_w_qkv': w(ks[10], (no, D_MODEL, SWA_IN), D_MODEL),
        'swa_b_qkv': 0.02 * jax.random.normal(ks[11], (no, SWA_IN), f32),
        'swa_w_out': w(ks[12], (no, SWA_MIX, D_MODEL), SWA_MIX),
        'swa_q_gain': gain(ks[13], (no, HEAD_DIM)),
        'swa_k_gain': gain(ks[14], (no, HEAD_DIM)),
        'swa_sinks': 0.5 * jax.random.normal(ks[15], (no, SWA_Q_HEADS), f32),
    }

def reference(x, positions, norm_mix, norm_mlp, mlp_w_up, mlp_w_down, hyb_w_in, hyb_w_out,
              ret_gn_gain, dil_q_gain, dil_k_gain, swa_w_qkv, swa_b_qkv, swa_w_out,
              swa_q_gain, swa_k_gain, swa_sinks):
    for layer in range(DEPTH):
        i = layer // 2
        h = rmsnorm(x, norm_mix[layer])
        if layer % 2 == 0:
            x = x + even_mixer(h, positions, hyb_w_in[i], hyb_w_out[i], ret_gn_gain[i],
                               dil_q_gain[i], dil_k_gain[i])
        else:
            x = x + swa_mixer(h, positions, swa_w_qkv[i], swa_b_qkv[i], swa_w_out[i],
                              swa_q_gain[i], swa_k_gain[i], swa_sinks[i])
        h = rmsnorm(x, norm_mlp[layer])
        x = x + sq_relu_mlp(h, mlp_w_up[layer], mlp_w_down[layer])
    return x


_drawn_inputs = setup_inputs


def setup_inputs(seed=0):
    import zlib

    import numpy as np

    out = dict(_drawn_inputs(seed))
    spreads = {}
    factors = {'dil_q_gain': 8.0,
     'dil_k_gain': 8.0,
     'swa_b_qkv': 4.686,
     'swa_q_gain': 8.0,
     'swa_k_gain': 8.0,
     'swa_sinks': 200.0}
    for name, (base, spread) in spreads.items():
        noise = np.random.default_rng([zlib.crc32(name.encode()), seed]).standard_normal(out[name].shape)
        drawn = base * np.exp(spread * noise) if base else spread * noise
        out[name] = __import__('jax').numpy.asarray(drawn.astype(out[name].dtype))
    for name, factor in factors.items():
        out[name] = (out[name] * factor).astype(out[name].dtype)
    return out
```

```python
import math

import concourse.bass as bass
from concourse import mybir
from contextlib import ExitStack


class Steps:

    def __init__(self, eng, sem):
        self.eng, self.sem, self.base, self.n = eng, sem, 0, 0

    def did(self, ins):
        ins.then_inc(self.sem, 1)
        self.n += 1

    def wait(self):
        self.eng.wait_ge(self.sem, self.base + self.n)

    def enter(self, it, per):
        self.saved, self.per = self.base + self.n, per
        self.base, self.n = self.saved + it * per, 0

    def leave(self, times):
        assert self.n == self.per, (self.n, self.per)
        self.base, self.n = self.saved + times * self.per, 0


def hybrid_trunk(nc, x_in, positions, norm_mix, norm_mlp, w_up, w_down, w_in, w_out0, gn_gain, dq_gain, dk_gain,
                 w_qkv, b_qkv, w_out1, sq_gain, sk_gain, sinks, out, x_spill):
    f32, f32r, i32 = mybir.dt.float32, mybir.dt.float32r, mybir.dt.int32
    ALU = mybir.AluOpType
    ACT = mybir.ActivationFunctionType
    AX = mybir.AxisListType

    P = 128
    S, D = x_in.shape[1], x_in.shape[2]
    T = S // P
    KD = D // P
    FF = w_up.shape[2]
    EPS = 1e-6
    HD = 64
    W = 384
    RH, RV = 4, 128
    HALF_R, HALF_D = HD // 2, HD // 8
    NG = 4
    OUTW = (384, 384, 256)
    FC = 256
    NC = FF // FC
    BIG = 1e30
    QSCALE = -(HD ** -0.5)
    GEMM_BANKS, U_BANKS, D_BANKS = 2, 4, 4
    LG = [math.log1p(-(2.0 ** (-5.0 - h))) for h in range(RH)]

    G_R, G_D, G_O0, G_S, G_O1 = 0, NG, 2 * NG, 2 * NG + 3, 3 * NG + 3
    L_R, L_D, L_O0 = 0, NG, 2 * NG
    L_M0 = 2 * NG + 3
    L_S = L_M0 + 2 * NC
    L_O1 = L_S + NG
    L_M1 = L_O1 + 3

    ctx = ExitStack()
    with ctx:
        def sb(name, shape, dt=f32):
            return ctx.enter_context(nc.sbuf_tensor(name, shape, dt))

        def ps(name, shape):
            return ctx.enter_context(nc.psum_tensor(name, shape, f32))

        def sem(name):
            return ctx.enter_context(nc.semaphore(name))

        hT_hi = sb("hT_hi", [P, KD, S], f32r)
        hT_lo = sb("hT_lo", [P, KD, S], f32r)
        W_hi = sb("W_hi", [P, 2, KD * W], f32r)
        W_lo = sb("W_lo", [P, 2, KD * W], f32r)
        raw = sb("raw", [P, 2, 4 * W])
        X = sb("X", [P, T, D])
        nlm = sb("nlm", [P, T * P])
        cosR = sb("cosR", [P, T, HALF_R])
        sinR = sb("sinR", [P, T, HALF_R])
        cosD = sb("cosD", [P, T, HALF_D])
        sinD = sb("sinD", [P, T, HALF_D])
        ident = sb("ident", [P, P])
        gainD = sb("gainD", [P, 4, HD])
        c1 = sb("c1", [P, 1024])
        decay = c1[:, 0:RH * P].rearrange("p (h q) -> p h q", h=RH)
        gnB = c1[:, RH * P:2 * RH * P]
        swm = c1[:, 0:256]
        gainS = c1[:, 256:256 + 5 * HD].rearrange("p (h d) -> p h d", h=5)
        biasS = c1[:, 576:576 + W]
        sq = sb("sq", [P, 5 * HD])
        ropeA = sb("ropeA", [P, 5 * 16])
        ropeB = sb("ropeB", [P, 5 * 16])
        st = sb("st", [P, 128])
        neghalf = st[:, 0:8]
        ss = st[:, 8:16]
        rstd = st[:, 16:24]
        xi = st[:, 24:28]
        zeta = st[:, 28:32]
        cdec = st[:, 32:36]
        negm = st[:, 36:44]
        den = st[:, 44:52]
        rden = st[:, 52:60]
        nsink = st[:, 60:76]
        es = st[:, 76:80]
        bst = st[:, 80:86]
        bag = st[:, 86:90]
        A0 = nc.sbuf_base
        off = [A0]

        def at(name, shape, dt=f32, start=None):
            size = 4 * int(math.prod(shape[1:]))
            o = off[0] if start is None else start
            t = nc.alloc_sbuf_tensor_at(name, shape, dt, offset=o)
            if start is None:
                off[0] += size
            return t, o

        G, _ = at("G", [P, T, W])
        QK, _ = at("QK", [P, 2, W])
        kT, kT_at = at("kT", [P, S])
        qT, _ = at("qT", [P, 2, 2 * P])
        Pm, P_at = at("Pm", [P, 2, 1024])
        pT, pT_at = at("pT", [P, 2, 1024])
        end_mix = off[0]
        xn, _ = at("xn", [P, 2, D], start=P_at)
        gB, _ = at("gB", [P, D], start=pT_at)
        junk, _ = at("junk", [P, D], start=pT_at + 4 * D)
        off[0] = P_at
        rA, _ = at("rA", [P, 2 * HD])
        rB, _ = at("rB", [P, 2 * HD])
        rsT, _ = at("rsT", [P, 2, P])
        rR, _ = at("rR", [HD, 2, RV])
        rsg, _ = at("rsg", [P, 2, RV])
        re, _ = at("re", [P, 2, RV])
        rt, _ = at("rt", [P, 2, RV])
        assert off[0] <= end_mix
        off[0] = A0
        a_hi, _ = at("a_hi", [P, 2, 2, S], f32r)
        a_lo, _ = at("a_lo", [P, 2, 2, S], f32r)
        r2, _ = at("r2", [P, 2, 512])
        assert off[0] <= end_mix
        off[0] = kT_at
        posi, _ = at("posi", [P, T], i32)
        posf, _ = at("posf", [P, T])
        invt, _ = at("invt", [P, HALF_R + HALF_D])
        ang, _ = at("ang", [P, T, HALF_R + HALF_D])
        nn, _ = at("nn", [P, T, HALF_R + HALF_D])
        off[0] = P_at
        di, _ = at("di", [P, T * P], i32)
        df, _ = at("df", [P, T * P])
        Gflat = G[:, :, :].rearrange("p a b -> p (a b)")
        t1, t2 = Gflat[:, T * P:2 * T * P], Gflat[:, 2 * T * P:3 * T * P]
        di4 = Gflat[:, 0:T * P].bitcast(i32)
        assert end_mix <= nc.sbuf_usable_end, end_mix

        gp = ps("gp", [P, 2, 512])
        sc = ps("sc", [P, 1024])
        tp = ps("tp", [P, 1024])
        o_ps = ps("o_ps", [P, 512])
        qt = ps("qt", [P, 512])
        u_out = [gp[:, 0, :], gp[:, 1, :], sc[:, 0:512], sc[:, 512:1024]]
        d_out = [tp[:, 0:512], tp[:, 512:1024], o_ps[:, :], qt[:, :]]
        nt_out = [sc, tp]
        o_out = [o_ps, qt]

        raw_full = [sem("raw_full0"), sem("raw_full1")]
        w_hi = sem("w_hi")
        w_ready = sem("w_ready")
        x_full = [sem(f"x_full{i}") for i in range(T)]
        const_in = sem("const_in")
        gB_full = sem("gB_full")
        c1_full = sem("c1_full")
        spilled = sem("spilled")
        stored = sem("stored")
        aside = sem("aside")
        phase = sem("phase")
        act_step, dve_step, pool_step = sem("act_step"), sem("dve_step"), sem("pool_step")
        ss_ready, rstd_ready, xn_ready, nt_done, ht_hi, ht_ready = [
            sem(n) for n in ("ss_ready", "rstd_ready", "xn_ready", "nt_done", "ht_hi", "ht_ready")]
        gemm_done, gemm_evac = sem("gemm_done"), sem("gemm_evac")
        x_sum = sem("x_sum")
        r_exp, r_qk, r_qt, r_qtev, r_st, r_u, r_sT, r_R, r_o, r_var, r_rstd, r_x = [
            sem(n) for n in ("r_exp", "r_qk", "r_qt", "r_qtev", "r_st", "r_u", "r_sT", "r_R", "r_o", "r_var",
                             "r_rstd", "r_x")]
        h_ss, h_rstd, qk_ready, qt_done, qkt_ready, s_done, sm_ready, p_ready, tp_done, pt_ready, pv_done, o_evac = [
            sem(n) for n in ("h_ss", "h_rstd", "qk_ready", "qt_done", "qkt_ready", "s_done", "sm_ready", "p_ready",
                             "tp_done", "pt_ready", "pv_done", "o_evac")]
        u_done, u_evac, a_sq, a_hi_done, a_ready, d_done, d_evac = [
            sem(n) for n in ("u_done", "u_evac", "a_sq", "a_hi_done", "a_ready", "d_done", "d_evac")]

        def alone(eng):
            eng.sem_inc(aside, 1)

        def barrier(eng, k):
            eng.drain().then_inc(phase, 1)
            eng.wait_ge(phase, 4 * k)

        per = {"R": 64, "D": 48, "O": 16, "S": 48, "M": 16}
        F_R = 0
        F_D = F_R + NG * per["R"]
        F_O0 = F_D + NG * per["D"]
        F_M0 = F_O0 + 3 * per["O"]
        F_S = F_M0 + 2 * NC * per["M"]
        F_O1 = F_S + NG * per["S"]
        F_M1 = F_O1 + 3 * per["O"]

        def l_up(c):
            return 0 if isinstance(c, int) and c == 0 else 2 if isinstance(c, int) and c == 1 else 2 * c - 1

        def l_down(c):
            return 1 if isinstance(c, int) and c == 0 else 2 * NC - 1 if isinstance(c, int) and c == NC - 1 else 2 * c + 2

        block = ctx.enter_context(nc.Block())

        @block.sync
        def _(sp):
            def free(L, p):
                if not (isinstance(L, int) and L == 0):
                    sp.wait_ge(w_ready, 2 * L - 1 + p)

            def rawp(p, n):
                return raw[:, p, 0:4 * n].rearrange("q (d n) -> q d n", d=4)

            def rows(w, p):
                return w.rearrange("(d q) n -> q d n", q=P)[:, 4 * p:4 * p + 4, :]

            def runs(w, parts, L):
                for p in range(2):
                    free(L, p)
                    for c, n, first, start in parts:
                        sp.dma_start(rawp(p, W)[:, :, c:c + n],
                                     rows(w, p)[:, :, bass.ds(first + start, n)]).then_inc(raw_full[p], 16)

            def load_R(h, L):
                v = 2 * RH * HD
                runs(w_in[0], [(0, HD, 0, h * HD), (HD, HD, RH * HD, h * HD), (2 * HD, RV, v, h * RV),
                               (2 * HD + RV, RV, v + RH * RV, h * RV)], L)

            def load_D(g, L):
                runs(w_in[0], [(c * 2 * HD, 2 * HD, 2 * RH * HD + 2 * RH * RV + c * 8 * HD, g * 2 * HD) for c in range(3)], L)

            def load_S(g, L):
                runs(w_qkv[0], [(0, 4 * HD, 0, g * 4 * HD), (4 * HD, HD, D, g * HD), (5 * HD, HD, D + 4 * HD, g * HD)], L)

            def load_out(w, L):
                c = 0
                for j, n in enumerate(OUTW):
                    for p in range(2):
                        free(L + j, p)
                        sp.dma_start(rawp(p, n), rows(w, p)[:, :, c:c + n]).then_inc(raw_full[p], 16)
                    c += n

            def load_up(l, c, L):
                for p in range(2):
                    free(L, p)
                    sp.dma_start(rawp(p, FC), rows(w_up[l], p)[:, :, bass.ds(c * FC, FC)]).then_inc(raw_full[p], 16)

            def load_down(l, c, L):
                src = w_down[l].rearrange("(c q) n -> q c n", q=P)
                for p in range(2):
                    free(L, p)
                    sp.dma_start(raw[:, p, 0:D].rearrange("q (o n) -> q o n", o=1),
                                 src[:, bass.ds(c * 2 + p, 1), :]).then_inc(raw_full[p], 16)

            def load_mlp(l, LM):
                load_up(l, 0, LM + l_up(0))
                load_down(l, 0, LM + l_down(0))
                load_up(l, 1, LM + l_up(1))
                with sp.Fori(0, NC - 2) as c:
                    load_up(l, c + 2, LM + 3 + 2 * c)
                    load_down(l, c + 1, LM + 4 + 2 * c)
                load_down(l, NC - 1, LM + l_down(NC - 1))

            def bcast(v, n):
                return v.rearrange("(o n) -> o n", o=1).to_broadcast([P, n])

            xt = x_in[0].rearrange("(t q) d -> q t d", q=P)
            sp.dma_start(posi[:, :], positions[0].rearrange("(t q) -> q t", q=P),
                         allow_slow_non_contiguous=True).then_inc(const_in, 16)
            sp.dma_start(X[:, 0, :], xt[:, 0, :]).then_inc(x_full[0], 16)
            sp.dma_start(gB[:, :], bcast(norm_mix[0], D)).then_inc(gB_full, 16)
            for i in range(1, T):
                sp.dma_start(X[:, i, :], xt[:, i, :]).then_inc(x_full[i], 16)
            for n in range(2):
                sp.dma_start(gainD[:, n, :], bcast(dq_gain[0], HD)).then_inc(const_in, 16)
                sp.dma_start(gainD[:, 2 + n, :], bcast(dk_gain[0], HD)).then_inc(const_in, 16)
            sp.dma_start(gnB, bcast(gn_gain[0].rearrange("h d -> (h d)"), RH * RV)).then_inc(const_in, 16)
            sp.dma_start(nsink, bcast(sinks[0], 16)).then_inc(const_in, 16)
            load_R(0, 0)
            with sp.Fori(1, NG) as h:
                load_R(h, h)
            with sp.Fori(0, NG) as g:
                load_D(g, g + L_D)
            load_out(w_out0[0], L_O0)

            def reload(src, k):
                for i in range(T):
                    sp.wait_ge(nt_done, k + i + 1)
                    sp.dma_start(X[:, i, :], src[:, i, :]).then_inc(x_full[i], 16)

            reload(xt, T)
            sp.wait_ge(phase, 4 * PH_D)
            sp.dma_start(gB[:, :], bcast(norm_mlp[0], D)).then_inc(gB_full, 16)
            load_mlp(0, L_M0)
            sp.wait_ge(phase, 4 * PH_M0)
            sp.dma_start(gB[:, :], bcast(norm_mix[1], D)).then_inc(gB_full, 16)
            spill = x_spill.rearrange("(t q) d -> q t d", q=P)
            for i in range(T):
                sp.dma_start(spill[:, i, :], X[:, i, :]).then_inc(spilled, 16)
            for n in range(4):
                sp.dma_start(gainS[:, n, :], bcast(sq_gain[0], HD)).then_inc(c1_full, 16)
            sp.dma_start(gainS[:, 4, :], bcast(sk_gain[0], HD)).then_inc(c1_full, 16)

            def load_bias(g):
                b = b_qkv[0]
                sp.dma_start(biasS[:, 0:4 * HD],
                             b[0:D].rearrange("(o n) -> o n", o=1)[:, bass.ds(g * 4 * HD, 4 * HD)].to_broadcast([P, 4 * HD])).then_inc(c1_full, 16)
                for n in range(2):
                    part = b[D + n * 4 * HD:D + (n + 1) * 4 * HD].rearrange("(o n) -> o n", o=1)
                    sp.dma_start(biasS[:, (4 + n) * HD:(5 + n) * HD],
                                 part[:, bass.ds(g * HD, HD)].to_broadcast([P, HD])).then_inc(c1_full, 16)

            load_bias(0)
            load_S(0, L_S)
            with sp.Fori(1, NG) as g:
                load_S(g, g + L_S)
                sp.wait_ge(gemm_evac, (g + G_S) * T + GEMM_BANKS)
                load_bias(g)
            load_out(w_out1[0], L_O1)
            sp.wait_ge(spilled, 16 * T)
            reload(spill, 4 * T)
            sp.wait_ge(phase, 4 * PH_S)
            sp.dma_start(gB[:, :], bcast(norm_mlp[1], D)).then_inc(gB_full, 16)
            load_mlp(1, L_M1)
            ot = out[0].rearrange("(t q) d -> q t d", q=P)
            for i in range(T):
                sp.wait_ge(d_evac, D_BANKS + 2 * 16 * NC - 16 + 2 * i + 2)
                sp.dma_start(ot[:, i, :], X[:, i, :]).then_inc(stored, 16)
            sp.wait_ge(stored, 16 * T)

        @block.tensor
        def _(pe):
            mm = nc.tensor.matmul

            def three(o, a, b, first, last):
                mm(o, a[0], b[0], start=first, stop=False)
                mm(o, a[0], b[1], start=False, stop=False)
                return mm(o, a[1], b[0], start=False, stop=last)

            def norm_T(src, i, k, ready):
                b = nt_out[i % 2]
                ready()
                if i >= 2:
                    pe.wait_ge(ht_ready, k + i - 1)
                for d in range(KD):
                    last = nc.tensor.transpose(b[:, d * P:(d + 1) * P], src[:, d * P:(d + 1) * P], ident[:, :])
                last.then_inc(nt_done, 1)

            def norm_phase(k):
                for i in range(T):
                    norm_T(xn[:, i % 2, :], i, k, lambda: pe.wait_ge(xn_ready, k_xn[k] + i + 1))

            def mix_phase(k):
                for i in range(T):
                    norm_T(X[:, i, :], i, k, lambda: None)

            def gemm_parts(n, slot, i, width, L, k):
                o = gp[:, i % 2, 0:width]
                for part in range(4):
                    if part == 0:
                        pe.wait_ge(gemm_evac, n + 1)
                        pe.wait_ge(ht_ready, k + i + 1)
                        if i == 0:
                            pe.wait_ge(w_ready, 2 * L + 2)
                    for d in (2 * part, 2 * part + 1):
                        c = slice(i * P, (i + 1) * P)
                        w = slice(d * width, (d + 1) * width)
                        last = three(o, (hT_hi[:, d, c], hT_lo[:, d, c]), (W_hi[:, slot, w], W_lo[:, slot, w]),
                                     d == 0, d == KD - 1)
                    if part == 3:
                        last.then_inc(gemm_done, 1)
                    yield

            def nothing():
                while True:
                    yield

            def ret_group(h, slot):
                for t in range(T + 1):
                    g = gemm_parts((h + G_R) * T + t, slot, t, W, h + L_R, 0) if t < T else nothing()
                    a, n = t - 1, h * T + t - 1
                    next(g)
                    next(g)
                    if t >= 1:
                        pe.wait_ge(r_qk, n + 1)
                        alone(pe)
                        for m in range(3):
                            last = nc.tensor.transpose(qt[0:HD, m * P:(m + 1) * P], QK[:, a % 2, m * HD:(m + 1) * HD],
                                                       ident[:, :])
                        last.then_inc(r_qt, 1)
                    next(g)
                    if t >= 1:
                        q = qT[:, :, :].rearrange("p a b -> p (a b)") if a % 2 == 0 else kT[:, :]
                        v = G[:, a, 2 * HD:2 * HD + RV]
                        pe.wait_ge(r_qtev, n + 1)
                        mm(sc[:, 0:P], q[0:HD, P:2 * P], q[0:HD, 0:P], start=True, stop=True).then_inc(r_st, 1)
                        mm(sc[0:HD, 512:512 + RV], QK[:, a % 2, 3 * HD:4 * HD], v, start=True, stop=True).then_inc(r_u, 1)
                    next(g)
                    if t >= 1:
                        pe.wait_ge(r_sT, n + 1)
                        o = o_ps[:, 0:RV]
                        last = mm(o, rsT[:, a % 2, :], v, start=True, stop=(a == 0))
                        if a >= 1:
                            pe.wait_ge(r_R, n)
                            last = mm(o, q[0:HD, 2 * P:3 * P], rR[:, a % 2, :], start=False, stop=True)
                        last.then_inc(r_o, 1)

            def att_group(kind, qa, gn, slot, L, k):
                def scores(a, j):
                    n = qa * 16 + 2 * a + j
                    if j == 0:
                        pe.wait_ge(qkt_ready, qa * T + a + 1)
                    else:
                        pe.wait_ge(sm_ready, n)
                    if kind == "D":
                        r = slice(HD * j, HD * (j + 1))
                        for c in range(0, (a + 1) * P, 512):
                            e = min(c + 512, (a + 1) * P)
                            last = mm(sc[:, c:e], qT[r, a % 2, 0:P], kT[r, c:e], start=True, stop=True)
                    else:
                        k0 = max(a - 1, 0) * P
                        for e in range(2):
                            r = slice(HD * e, HD * (e + 1))
                            last = mm(sc[:, e * 512:e * 512 + (a + 1) * P - k0], qT[r, a % 2, j * P:(j + 1) * P],
                                      kT[r, k0:(a + 1) * P], start=True, stop=True)
                    last.then_inc(s_done, 1)

                def blocks(a):
                    if kind == "D":
                        return [(c * P, c * P, c, 0) for c in range(a + 1)]
                    ks = [a] if a == 0 else [a - 1, a]
                    return [(e * 256 + m * P, (e * len(ks) + m) * P, c, e) for e in range(2) for m, c in enumerate(ks)]

                def trans(a, j):
                    pe.wait_ge(p_ready, qa * 16 + 2 * a + j + 1)
                    base = 512 * j if kind == "S" else 0
                    for c, to, _, _ in blocks(a):
                        last = nc.tensor.transpose(tp[:, base + to:base + to + P], Pm[:, j, c:c + P], ident[:, :])
                    last.then_inc(tp_done, 1)

                def values(a, j):
                    pe.wait_ge(pt_ready, qa * 16 + 2 * a + j + 1)
                    bl = blocks(a)
                    v0 = 4 * HD + HD * j if kind == "D" else 5 * HD
                    for m, (_, to, c, e) in enumerate(bl):
                        o = o_out[j][:, e * HD:(e + 1) * HD]
                        last = mm(o, pT[:, j, to:to + P], G[:, c, v0:v0 + HD],
                                  start=(m == 0 or bl[m - 1][3] != e), stop=(m == len(bl) - 1 or bl[m + 1][3] != e))
                    last.then_inc(pv_done, 1)

                for t in range(T + 2):
                    g = gemm_parts(gn * T + t, slot, t, W, L, k) if t < T else nothing()
                    a, b = t - 1, t - 2
                    next(g)
                    if b >= 0:
                        values(b, 0)
                        trans(b, 1)
                    next(g)
                    if b >= 0:
                        values(b, 1)
                    if 0 <= a < T:
                        pe.wait_ge(qk_ready, qa * T + a + 1)
                        for m in range(2 if kind == "D" else 3):
                            last = nc.tensor.transpose(sc[:, m * P:(m + 1) * P], QK[:, a % 2, m * P:(m + 1) * P],
                                                       ident[:, :])
                        last.then_inc(qt_done, 1)
                    next(g)
                    if 0 <= a < T:
                        scores(a, 0)
                    next(g)
                    if 0 <= a < T:
                        scores(a, 1)
                        trans(a, 0)

            def out_proj(gn, L, k):
                for j, n in enumerate(OUTW):
                    for i in range(T):
                        for _ in gemm_parts((gn + j) * T + i, (L + j) % 2, i, n, L + j, k):
                            pass

            def up(m, c, par, l, LU):
                pe.wait_ge(w_ready, 2 * LU + 2)
                su = (L_M0 if l == 0 else L_M1) % 2
                for sh in range(2):
                    for ft in range(2):
                        n = m * 4 * NC + 4 * c + 2 * sh + ft
                        o = u_out[2 * sh + ft]
                        if not (isinstance(c, int) and c > 1):
                            pass
                        pe.wait_ge(u_evac, n + 1)
                        for d in range(KD):
                            w = slice(d * FC + ft * P, d * FC + (ft + 1) * P)
                            r = slice(sh * 512, (sh + 1) * 512)
                            last = three(o, (W_hi[:, su, w], W_lo[:, su, w]), (hT_hi[:, d, r], hT_lo[:, d, r]),
                                         d == 0, d == KD - 1)
                        last.then_inc(u_done, 1)

            def down(m, c, par, l, LD):
                pe.wait_ge(w_ready, 2 * LD + 2)
                pe.wait_ge(a_ready, m * 4 * NC + 4 * c + 4)
                sd = 1 - (L_M0 if l == 0 else L_M1) % 2
                for i in range(T):
                    for nh in range(2):
                        n = m * 16 * NC + 16 * c + 2 * i + nh
                        o = d_out[(2 * i + nh) % D_BANKS]
                        pe.wait_ge(d_evac, n + 1)
                        for ft in range(2):
                            r = slice(i * P, (i + 1) * P)
                            w = slice(ft * D + nh * 512, ft * D + (nh + 1) * 512)
                            last = three(o, (a_hi[:, par, ft, r], a_lo[:, par, ft, r]),
                                         (W_hi[:, sd, w], W_lo[:, sd, w]), ft == 0, ft == 1)
                        last.then_inc(d_done, 1)

            def mlp(l, LM):
                up(l, 0, 0, l, LM + l_up(0))
                up(l, 1, 1, l, LM + l_up(1))
                down(l, 0, 0, l, LM + l_down(0))
                with pe.Fori(0, NC // 2 - 1) as q:
                    up(l, 2 * q + 2, 0, l, LM + 4 * q + 3)
                    down(l, 2 * q + 1, 1, l, LM + 4 * q + 4)
                    up(l, 2 * q + 3, 1, l, LM + 4 * q + 5)
                    down(l, 2 * q + 2, 0, l, LM + 4 * q + 6)
                down(l, NC - 1, 1, l, LM + l_down(NC - 1))

            pe.sem_inc(gemm_evac, GEMM_BANKS)
            pe.sem_inc(u_evac, U_BANKS)
            pe.sem_inc(d_evac, D_BANKS)
            barrier(pe, PH_SETUP)
            norm_phase(0)
            barrier(pe, PH_N0)
            with pe.Fori(0, NG // 2) as q:
                for u in range(2):
                    ret_group(2 * q + u, (L_R + u) % 2)
            barrier(pe, PH_R)
            with pe.Fori(0, NG // 2) as q:
                for u in range(2):
                    att_group("D", 2 * q + u, 2 * q + u + G_D, (L_D + u) % 2, 2 * q + u + L_D, 0)
            barrier(pe, PH_D)
            mix_phase(T)
            out_proj(G_O0, L_O0, T)
            barrier(pe, PH_O0)
            norm_phase(2 * T)
            barrier(pe, PH_N1)
            mlp(0, L_M0)
            barrier(pe, PH_M0)
            norm_phase(3 * T)
            barrier(pe, PH_N2)
            with pe.Fori(0, NG // 2) as q:
                for u in range(2):
                    att_group("S", 2 * q + u + NG, 2 * q + u + G_S, (L_S + u) % 2, 2 * q + u + L_S, 3 * T)
            barrier(pe, PH_S)
            mix_phase(4 * T)
            out_proj(G_O1, L_O1, 4 * T)
            barrier(pe, PH_O1)
            norm_phase(5 * T)
            barrier(pe, PH_N3)
            mlp(1, L_M1)
            barrier(pe, PH_M1)

        @block.scalar
        def _(act):
            A = nc.scalar.activation
            step = Steps(act, act_step)

            def split_hi(L, p, slot, width, full):
                act.wait_ge(raw_full[p], full)
                A(W_hi[:, slot, 4 * p * width:4 * (p + 1) * width], raw[:, p, 0:4 * width], ACT.Copy).then_inc(w_hi, 1)

            def norm_phase(m, k):
                for i in range(T + 1):
                    if i < T:
                        if m == 0:
                            act.wait_ge(x_full[i], 16)
                        if i >= 1:
                            act.wait_ge(ss_ready, m * T + i)
                        A(junk[:, :], X[:, i, :], ACT.Square, accum_out=ss[:, i:i + 1]).then_inc(ss_ready, 1)
                    if i >= 1:
                        copy_T(i - 1, k)

            def copy_T(i, k):
                act.wait_ge(nt_done, k + i + 1)
                A(hT_hi[:, :, i * P:(i + 1) * P], nt_out[i % 2][:, :].rearrange("p (d c) -> p d c", d=KD),
                  ACT.Copy).then_inc(ht_hi, 1)

            def evac(n, i):
                act.wait_ge(gemm_done, n + 1)
                A(G[:, i, :], gp[:, i % 2, 0:W], ACT.Copy).then_inc(gemm_evac, 1)

            def ret_group(h, slot, full):
                for t in range(T + 1):
                    a, n = t - 1, h * T + t - 1
                    if t >= 1:
                        q = qT[:, :, :].rearrange("p a b -> p (a b)") if a % 2 == 0 else kT[:, :]
                        act.wait_ge(r_qt, n + 1)
                        A(q[0:HD, 0:3 * P], qt[0:HD, 0:3 * P], ACT.Copy).then_inc(r_qtev, 1)
                    if t < T:
                        evac(h * T + t, t)
                        act.wait_ge(gemm_evac, h * T + t + 1 + GEMM_BANKS)
                        A(re[:, t % 2, :], G[:, t, 2 * HD + RV:W], ACT.Exp, scale=-1.0).then_inc(r_exp, 1)
                    if t in (2, 5):
                        split_hi(h + 1, t // 4, 1 - slot, W, full[t // 4])
                act.wait_ge(r_x, (h + 1) * T)

            def att_group(kind, qa, gn, slot, L, full):
                for t in range(T + 2):
                    a, b = t - 1, t - 2
                    if b >= 0:
                        for j in range(2):
                            n = qa * 16 + 2 * b + j
                            w = (b + 1) * P if kind == "D" else (2 * P if b == 0 else 4 * P)
                            act.wait_ge(tp_done, n + 1)
                            base = 512 * j if kind == "S" else 0
                            A(pT[:, j, 0:w], tp[:, base:base + w], ACT.Copy).then_inc(pt_ready, 1)
                    if 0 <= a < T:
                        act.wait_ge(qt_done, qa * T + a + 1)
                        m = 1 if kind == "D" else 2
                        A(qT[:, a % 2, 0:m * P], sc[:, 0:m * P], ACT.Copy)
                        A(kT[:, a * P:(a + 1) * P], sc[:, m * P:(m + 1) * P], ACT.Copy).then_inc(qkt_ready, 1)
                    for j in range(2):
                        if 0 <= a < T:
                            n = qa * 16 + 2 * a + j
                            act.wait_ge(sm_ready, n + 1)
                            if kind == "D":
                                w = (a + 1) * P
                                A(Pm[:, j, 0:w], Pm[:, j, 0:w], ACT.Exp, scale=-1.0, bias=negm[:, j:j + 1],
                                  accum_out=den[:, j:j + 1]).then_inc(p_ready, 1)
                            else:
                                w = P if a == 0 else 2 * P
                                A(es[:, 2 * j:2 * j + 2], es[:, 2 * j:2 * j + 2], ACT.Exp)
                                for e in range(2):
                                    z = slice(2 * j + e, 2 * j + e + 1)
                                    last = A(Pm[:, j, e * 256:e * 256 + w], Pm[:, j, e * 256:e * 256 + w], ACT.Exp,
                                             scale=-1.0, bias=negm[:, z], accum_out=den[:, z])
                                last.then_inc(p_ready, 1)
                        if j == 0 and t < T and kind == "D":
                            evac(gn * T + t, t)
                    if t in (2, 5):
                        split_hi(L + 1, t // 4, 1 - slot, W, full[t // 4])
                act.wait_ge(pv_done, (qa + 1) * 16)

            def out_phase(gn, L, F, k, FM):
                for i in range(T):
                    copy_T(i, k)
                for j in range(1, 3):
                    if j == 2:
                        act.wait_ge(gemm_done, (gn + 1) * T)
                    for p in range(2):
                        split_hi(L + j, p, (L + j) % 2, OUTW[j], F + 16 * (j + 1))
                act.wait_ge(gemm_done, (gn + 2) * T)
                split_up(L + 3, (L + 3) % 2, FM + 16)

            def split_up(L, su, full):
                for p in range(2):
                    split_hi(L, p, su, FC, full)

            def split_down(L, sd, full):
                for p in range(2):
                    act.wait_ge(raw_full[p], full)
                    A(W_hi[:, sd, p * D:(p + 1) * D], raw[:, p, 0:D], ACT.Copy).then_inc(w_hi, 1)

            def hidden(m, c, par):
                for sh in range(2):
                    for ft in range(2):
                        n = m * 4 * NC + 4 * c + 2 * sh + ft
                        act.wait_ge(u_done, n + 1)
                        if not (isinstance(n, int) and n < 2):
                            act.wait_ge(a_ready, n - 1)
                        A(r2[:, ft, :], u_out[2 * sh + ft], ACT.Relu).then_inc(u_evac, 1)
                        act.wait_ge(a_sq, n + 1)
                        A(a_hi[:, par, ft, sh * 512:(sh + 1) * 512], r2[:, ft, :], ACT.Copy).then_inc(a_hi_done, 1)

            def mlp(m, LM, FM):
                su = LM % 2
                sd = 1 - su
                split_down(LM + 1, sd, FM + 32)
                hidden(m, 0, 0)
                split_up(LM + 2, su, FM + 48)
                hidden(m, 1, 1)
                with act.Fori(0, NC // 2 - 1) as q:
                    for u in range(2):
                        split_up(LM + 3 + 4 * q + 2 * u, su, FM + 16 * (4 + 4 * q + 2 * u))
                        act.wait_ge(d_done, m * 16 * NC + (2 * q + u + 1) * 16)
                        split_down(LM + 4 + 4 * q + 2 * u, sd, FM + 16 * (5 + 4 * q + 2 * u))
                        hidden(m, 2 * q + u + 2, u)
                act.wait_ge(d_done, m * 16 * NC + (NC - 1) * 16)
                split_down(LM + 2 * NC - 1, sd, FM + 16 * 2 * NC)

            act.wait_ge(pool_step, SETUP_POOL)
            for h in range(RH):
                A(decay[:, h, :], df[:, 0:P], ACT.Exp, scale=LG[h])
                A(xi[:, h:h + 1], df[:, P:P + 1], ACT.Exp, scale=LG[h])
                A(zeta[:, h:h + 1], df[:, P + 1:P + 2], ACT.Exp, scale=LG[h])
                last = A(cdec[:, h:h + 1], df[:, P + 2:P + 3], ACT.Exp, scale=LG[h])
            step.did(last)
            act.wait_ge(dve_step, SETUP_SIN)
            A(sinR[:, :, :], ang[:, :, 0:HALF_R], ACT.Sin)
            A(sinD[:, :, :], ang[:, :, HALF_R:], ACT.Sin)
            A(cosR[:, :, :], nn[:, :, 0:HALF_R], ACT.Sin)
            step.did(A(cosD[:, :, :], nn[:, :, HALF_R:], ACT.Sin))
            barrier(act, PH_SETUP)
            for p in range(2):
                split_hi(0, p, 0, W, F_R + per["R"])
            norm_phase(0, 0)
            barrier(act, PH_N0)
            with act.Fori(0, NG // 2) as q:
                ret_group(2 * q, 0, [q * 2 * per["R"] + 2 * per["R"]] * 2)
                ret_group(2 * q + 1, 1, [q * (F_D + per["D"] - 3 * per["R"]) + 3 * per["R"]] * 2)
            barrier(act, PH_R)
            with act.Fori(0, NG // 2) as q:
                att_group("D", 2 * q, 2 * q + G_D, 0, 2 * q + L_D, [q * 2 * per["D"] + F_D + 2 * per["D"]] * 2)
                att_group("D", 2 * q + 1, 2 * q + 1 + G_D, 1, 2 * q + 1 + L_D,
                          [q * (F_O0 + per["O"] - F_D - 3 * per["D"]) + F_D + 3 * per["D"]] * 2)
            barrier(act, PH_D)
            out_phase(G_O0, L_O0, F_O0, T, F_M0)
            barrier(act, PH_O0)
            norm_phase(1, 2 * T)
            barrier(act, PH_N1)
            mlp(0, L_M0, F_M0)
            barrier(act, PH_M0)
            for p in range(2):
                split_hi(L_S, p, L_S % 2, W, F_S + per["S"])
            norm_phase(2, 3 * T)
            barrier(act, PH_N2)
            with act.Fori(0, NG // 2) as q:
                att_group("S", 2 * q + NG, 2 * q + G_S, L_S % 2, 2 * q + L_S, [q * 2 * per["S"] + F_S + 2 * per["S"]] * 2)
                att_group("S", 2 * q + 1 + NG, 2 * q + 1 + G_S, (L_S + 1) % 2, 2 * q + 1 + L_S,
                          [q * (F_O1 + per["O"] - F_S - 3 * per["S"]) + F_S + 3 * per["S"]] * 2)
            barrier(act, PH_S)
            out_phase(G_O1, L_O1, F_O1, 4 * T, F_M1)
            barrier(act, PH_O1)
            norm_phase(3, 5 * T)
            barrier(act, PH_N3)
            mlp(1, L_M1, F_M1)
            barrier(act, PH_M1)

        @block.vector
        def _(dve):
            V = nc.vector
            step = Steps(dve, dve_step)

            def setup():
                dve.wait_ge(const_in, 16 * 7)
                V.tensor_scalar(gainD[:, 0:2, :], gainD[:, 0:2, :], QSCALE, None, ALU.mult)
                V.tensor_scalar(nsink, nsink, -1.0, None, ALU.mult)
                step.did(V.tensor_copy(posf[:, :], posi[:, :]))
                dve.wait_ge(pool_step, SETUP_POOL)
                step.wait()
                n3 = [P, T, HALF_R + HALF_D]
                step.did(V.tensor_tensor(ang[:, :, :], posf[:, :].rearrange("p (t o) -> p t o", o=1).to_broadcast(n3),
                                         invt[:, :].rearrange("p (o n) -> p o n", o=1).to_broadcast(n3), ALU.mult))
                step.wait()
                magic = 1.5 * 2.0 ** 23
                step.did(V.tensor_scalar(nn[:, :, :], ang[:, :, :], 1.0 / (2 * math.pi), magic, ALU.mult, ALU.add))
                step.wait()
                step.did(V.tensor_scalar(nn[:, :, :], nn[:, :, :], magic, None, ALU.subtract))
                left = 2 * math.pi
                for bits in (5, 13, 21, None):
                    part = left if bits is None else math.floor(left * 2.0 ** bits) / 2.0 ** bits
                    left -= part
                    step.wait()
                    step.did(V.scalar_tensor_tensor(ang[:, :, :], nn[:, :, :], -part, ang[:, :, :], ALU.mult, ALU.add))
                step.wait()
                lim = 3.1415925
                step.did(V.tensor_scalar(ang[:, :, :], ang[:, :, :], lim, -lim, ALU.min, ALU.max))
                step.wait()
                step.did(V.tensor_scalar(nn[:, :, :], ang[:, :, :], -1.0, None, ALU.mult))
                step.wait()
                step.did(V.tensor_tensor(nn[:, :, :], nn[:, :, :], ang[:, :, :], ALU.max))
                step.wait()
                step.did(V.tensor_scalar(nn[:, :, :], nn[:, :, :], -1.0, math.pi / 2, ALU.mult, ALU.add))
                assert step.n == SETUP_SIN, step.n
                dve.wait_ge(act_step, 1)
                V.tensor_tensor(decay, decay, t1[:, 0:P].rearrange("p (o q) -> p o q", o=1).to_broadcast([P, RH, P]), ALU.mult)
                V.tensor_scalar(zeta, zeta, HD ** -0.5, None, ALU.mult)
                step.did(V.tensor_scalar(di4, di[:, :], 3, None, ALU.bitwise_and))
                step.wait()
                step.did(V.tensor_copy(df[:, :], di[:, :]))
                step.did(V.tensor_scalar(di[:, :], di[:, :], 15, None, ALU.bitwise_and))
                step.wait()
                step.did(V.tensor_scalar(t1[:, :], di4, 0.0, None, ALU.is_equal))
                step.did(V.tensor_scalar(t2[:, :], di[:, :], 0.0, None, ALU.is_equal))
                step.did(V.tensor_scalar(nlm[:, :], df[:, :], 128.0, None, ALU.is_le))
                step.wait()
                step.did(V.tensor_tensor(t2[:, :], t2[:, :], nlm[:, :], ALU.add))
                step.did(V.scalar_tensor_tensor(t1[:, :], df[:, :], 512.0, t1[:, :], ALU.is_le, ALU.mult))
                step.wait()
                step.did(V.tensor_tensor(t2[:, :], t2[:, :], t1[:, :], ALU.add))
                step.wait()
                step.did(V.scalar_tensor_tensor(t2[:, :], df[:, :], 0.0, t2[:, :], ALU.is_ge, ALU.mult))
                step.wait()
                step.did(V.tensor_scalar(nlm[:, :], t2[:, :], 0.0, BIG, ALU.is_equal, ALU.mult))
                for c in (2.0, 3.0):
                    step.wait()
                    step.did(V.tensor_scalar(t1[:, :], t2[:, :], c, -math.log(c), ALU.is_equal, ALU.mult))
                    step.wait()
                    step.did(V.tensor_tensor(nlm[:, :], nlm[:, :], t1[:, :], ALU.add))

            def lo_T(i, k):
                dve.wait_ge(ht_hi, k + i + 1)
                c = slice(i * P, (i + 1) * P)
                V.tensor_tensor(hT_lo[:, :, c], nt_out[i % 2][:, :].rearrange("p (d c) -> p d c", d=KD),
                                hT_hi[:, :, c].bitcast(f32), ALU.subtract).then_inc(ht_ready, 1)

            def norm_phase(m, k):
                dve.wait_ge(gB_full, 16 * (m + 1))
                for i in range(T + 1):
                    if i < T:
                        dve.wait_ge(rstd_ready, m * T + i + 1)
                        if i >= 2:
                            dve.wait_ge(nt_done, k + i - 1)
                        V.scalar_tensor_tensor(xn[:, i % 2, :], X[:, i, :], rstd[:, i:i + 1], gB[:, :], ALU.mult,
                                               ALU.mult).then_inc(xn_ready, 1)
                    if i >= 1:
                        lo_T(i - 1, k)

            def ret_rope(h, a):
                n = h * T + a
                dve.wait_ge(gemm_evac, n + 1 + GEMM_BANKS)
                x = G[:, a, 0:2 * HD].rearrange("p (m s d) -> p m s d", m=2, s=2)
                A4 = rA[:, :].rearrange("p (m s d) -> p m s d", m=2, s=2)
                B4 = rB[:, :].rearrange("p (m s d) -> p m s d", m=2, s=2)
                cc = cosR[:, a, :].rearrange("p (m s d) -> p m s d", m=1, s=1).to_broadcast([P, 2, 2, HALF_R])
                sn = sinR[:, a, :].rearrange("p (m d) -> p m d", m=1).to_broadcast([P, 2, HALF_R])
                step.did(V.tensor_tensor(A4, x, cc, ALU.mult))
                step.did(V.scalar_tensor_tensor(B4[:, :, 0, :], x[:, :, 1, :], -1.0, sn, ALU.mult, ALU.mult))
                step.did(V.tensor_tensor(B4[:, :, 1, :], x[:, :, 0, :], sn, ALU.mult))
                step.wait()
                q = QK[:, a % 2, :]
                step.did(V.tensor_tensor(q[:, 0:2 * HD], rA[:, :], rB[:, :], ALU.add))
                step.wait()
                step.did(V.tensor_scalar(q[:, 2 * HD:3 * HD], q[:, 0:HD], xi[:, bass.ds(h, 1)], None, ALU.mult))
                V.tensor_scalar(q[:, 3 * HD:4 * HD], q[:, HD:2 * HD], zeta[:, bass.ds(h, 1)], None,
                                ALU.mult).then_inc(r_qk, 1)
                dve.wait_ge(r_exp, n + 1)
                e, g = re[:, a % 2, :], rsg[:, a % 2, :]
                step.did(V.tensor_scalar(e, e, 1.0, None, ALU.add))
                step.wait()
                step.did(V.reciprocal(e, e))
                step.did(V.tensor_tensor(g, G[:, a, 2 * HD + RV:W], gnB[:, bass.ds(h * RV, RV)], ALU.mult))
                step.wait()
                step.did(V.tensor_tensor(g, g, e, ALU.mult))

            def ret_state(h, a):
                n = h * T + a
                dve.wait_ge(r_st, n + 1)
                V.tensor_tensor(rsT[:, a % 2, :], sc[:, 0:P], decay[:, bass.ds(h, 1), :].rearrange("p o q -> p (o q)"),
                                ALU.mult).then_inc(r_sT, 1)
                dve.wait_ge(r_u, n + 1)
                new = rR[:, (a + 1) % 2, :]
                if a == 0:
                    V.tensor_copy(new, sc[0:HD, 512:512 + RV]).then_inc(r_R, 1)
                else:
                    dve.wait_ge(r_R, n)
                    V.scalar_tensor_tensor(new, rR[:, a % 2, :], cdec[0:HD, bass.ds(h, 1)], sc[0:HD, 512:512 + RV],
                                           ALU.mult, ALU.add).then_inc(r_R, 1)

            def ret_out(h, a):
                n = h * T + a
                dve.wait_ge(r_o, n + 1)
                step.did(V.bn_stats(bst, o_ps[:, 0:RV]))
                step.wait()
                alone(dve)
                V.bn_aggr(bag[:, 0:2], bst).then_inc(r_var, 1)
                dve.wait_ge(r_rstd, n + 1)
                step.did(V.tensor_scalar(rt[:, a % 2, :], o_ps[:, 0:RV], bag[:, 0:1], bag[:, 2:3], ALU.subtract, ALU.mult))
                step.wait()
                V.tensor_tensor(X[:, a, bass.ds(h * RV, RV)], rt[:, a % 2, :], rsg[:, a % 2, :], ALU.mult).then_inc(r_x, 1)

            def ret_group(h):
                for t in range(T + 1):
                    if t >= 1:
                        ret_state(h, t - 1)
                    if t < T:
                        ret_rope(h, t)
                    if t >= 1:
                        ret_out(h, t - 1)

            def prep(kind, qa, gn, a):
                H = 4 if kind == "D" else 5
                n = qa * T + a
                dve.wait_ge(gemm_evac, gn * T + a + 1 + GEMM_BANKS)
                x = G[:, a, 0:H * HD].rearrange("p (h d) -> p h d", h=H)
                s3 = sq[:, 0:H * HD].rearrange("p (h d) -> p h d", h=H)
                q = QK[:, a % 2, 0:H * HD].rearrange("p (h d) -> p h d", h=H)
                step.did(V.tensor_tensor(s3, x, x, ALU.mult))
                step.wait()
                V.tensor_reduce(ss[:, 0:H], s3, AX.X, ALU.add).then_inc(h_ss, 1)
                step.did(V.tensor_tensor(q, x, gainD[:, :, :] if kind == "D" else gainS, ALU.mult))
                dve.wait_ge(h_rstd, n + 1)
                step.wait()
                rb = rstd[:, 0:H].rearrange("p (h o) -> p h o", o=1).to_broadcast([P, H, HD])
                step.did(V.tensor_tensor(q, q, rb, ALU.mult))
                A3 = ropeA[:, 0:H * 16].rearrange("p (h s d) -> p h s d", h=H, s=2)
                B3 = ropeB[:, 0:H * 16].rearrange("p (h s d) -> p h s d", h=H, s=2)
                q4 = q[:, :, 0:2 * HALF_D].rearrange("p h (s d) -> p h s d", s=2)
                cc = cosD[:, a, :].rearrange("p (m s d) -> p m s d", m=1, s=1).to_broadcast([P, H, 2, HALF_D])
                sn = sinD[:, a, :].rearrange("p (m d) -> p m d", m=1).to_broadcast([P, H, HALF_D])
                step.wait()
                step.did(V.tensor_tensor(A3, q4, cc, ALU.mult))
                step.did(V.scalar_tensor_tensor(B3[:, :, 0, :], q4[:, :, 1, :], -1.0, sn, ALU.mult, ALU.mult))
                step.did(V.tensor_tensor(B3[:, :, 1, :], q4[:, :, 0, :], sn, ALU.mult))
                step.wait()
                if kind == "D":
                    V.tensor_tensor(q4, A3, B3, ALU.add).then_inc(qk_ready, 1)
                else:
                    step.did(V.tensor_tensor(q4, A3, B3, ALU.add))
                    step.wait()
                    V.tensor_copy(QK[:, a % 2, 5 * HD:6 * HD], QK[:, a % 2, 4 * HD:5 * HD]).then_inc(qk_ready, 1)

            def maxima(kind, qa, a, j, g):
                n = qa * 16 + 2 * a + j
                dve.wait_ge(s_done, n + 1)
                alone(dve)
                if kind == "D":
                    w = (a + 1) * P
                    V.tensor_tensor_reduce(out=Pm[:, j, 0:w], in0=sc[:, 0:w], in1=nlm[:, (T - 1 - a) * P:T * P], scale=1.0,
                                           scalar=3e38, op0=ALU.add, op1=ALU.min, accum_out=negm[:, j:j + 1]).then_inc(sm_ready, 1)
                    return
                w = P if a == 0 else 2 * P
                for e in range(2):
                    z = 4 + 2 * j + e
                    step.did(V.tensor_tensor_reduce(out=Pm[:, j, e * 256:e * 256 + w], in0=sc[:, e * 512:e * 512 + w],
                                                    in1=swm[:, 256 - w:256], scale=1.0, scalar=3e38, op0=ALU.add,
                                                    op1=ALU.min, accum_out=negm[:, z:z + 1]))
                step.wait()
                sk = nsink[:, bass.ds(g * 4 + 2 * j, 2)]
                step.did(V.tensor_tensor(negm[:, 2 * j:2 * j + 2], negm[:, 4 + 2 * j:6 + 2 * j], sk, ALU.min))
                step.wait()
                V.tensor_tensor(es[:, 2 * j:2 * j + 2], negm[:, 2 * j:2 * j + 2], sk, ALU.subtract).then_inc(sm_ready, 1)

            def outputs(kind, qa, a, j, g):
                n = qa * 16 + 2 * a + j
                dve.wait_ge(p_ready, n + 1)
                if kind == "D":
                    step.did(V.reciprocal(rden[:, j:j + 1], den[:, j:j + 1]))
                    step.wait()
                    dve.wait_ge(pv_done, n + 1)
                    V.tensor_scalar(X[:, a, bass.ds(g * 2 * HD + D // 2 + j * HD, HD)], o_out[j][:, 0:HD],
                                    rden[:, j:j + 1], None, ALU.mult).then_inc(o_evac, 1)
                    return
                z = slice(2 * j, 2 * j + 2)
                step.did(V.tensor_tensor(den[:, z], den[:, z], es[:, z], ALU.add))
                step.wait()
                step.did(V.reciprocal(rden[:, z], den[:, z]))
                step.wait()
                dve.wait_ge(pv_done, n + 1)
                V.tensor_tensor(X[:, a, bass.ds(g * 4 * HD + 2 * j * HD, 2 * HD)].rearrange("p (e d) -> p e d", e=2),
                                o_out[j][:, 0:2 * HD].rearrange("p (e d) -> p e d", e=2),
                                rden[:, z].rearrange("p (e o) -> p e o", o=1).to_broadcast([P, 2, HD]), ALU.mult).then_inc(o_evac, 1)

            def att_group(kind, qa, gn, g):
                for t in range(T + 2):
                    a, b = t - 1, t - 2
                    if 0 <= a < T:
                        prep(kind, qa, gn, a)
                    if b >= 0:
                        outputs(kind, qa, b, 0, g)
                        outputs(kind, qa, b, 1, g)
                    if 0 <= a < T:
                        maxima(kind, qa, a, 0, g)
                    if t < T and kind == "S":
                        dve.wait_ge(gemm_done, gn * T + t + 1)
                        if t == 0:
                            dve.wait_ge(c1_full, g * 48 + 16 * 5 + 48)
                        V.tensor_tensor(G[:, t, :], gp[:, t % 2, 0:W], biasS, ALU.add).then_inc(gemm_evac, 1)
                    if 0 <= a < T:
                        maxima(kind, qa, a, 1, g)

            def out_phase(gn, k, m):
                c = 0
                for i in range(T):
                    lo_T(i, k)
                for j, n in enumerate(OUTW):
                    for i in range(T):
                        if j == 0:
                            dve.wait_ge(x_full[i], 16 * (m + 2 - m // 2 * 0) if m == 0 else 16 * 3)
                        dve.wait_ge(gemm_done, (gn + j) * T + i + 1)
                        V.tensor_tensor(X[:, i, c:c + n], gp[:, i % 2, 0:n], X[:, i, c:c + n], ALU.add).then_inc(gemm_evac, 1)
                    c += n

            def square(m, c):
                for sh in range(2):
                    for ft in range(2):
                        n = m * 4 * NC + 4 * c + 2 * sh + ft
                        dve.wait_ge(u_evac, n + 1 + U_BANKS)
                        V.tensor_tensor(r2[:, ft, :], r2[:, ft, :], r2[:, ft, :], ALU.mult).then_inc(a_sq, 1)

            def add_down(m, c):
                for i in range(T):
                    for nh in range(2):
                        n = m * 16 * NC + 16 * c + 2 * i + nh
                        dve.wait_ge(d_done, n + 1)
                        x = X[:, i, nh * 512:(nh + 1) * 512]
                        V.tensor_tensor(x, d_out[(2 * i + nh) % D_BANKS], x, ALU.add).then_inc(d_evac, 1)

            def mlp(m):
                square(m, 0)
                square(m, 1)
                with dve.Fori(0, NC - 2) as c:
                    add_down(m, c)
                    square(m, c + 2)
                add_down(m, NC - 2)
                add_down(m, NC - 1)

            setup()
            barrier(dve, PH_SETUP)
            norm_phase(0, 0)
            barrier(dve, PH_N0)
            with dve.Fori(0, NG // 2) as q:
                step.enter(q, 2 * T * 11)
                for u in range(2):
                    ret_group(2 * q + u)
                step.leave(NG // 2)
            barrier(dve, PH_R)
            with dve.Fori(0, NG // 2) as q:
                step.enter(q, 2 * T * 8)
                for u in range(2):
                    att_group("D", 2 * q + u, 2 * q + u + G_D, 2 * q + u)
                step.leave(NG // 2)
            barrier(dve, PH_D)
            out_phase(G_O0, T, 0)
            barrier(dve, PH_O0)
            norm_phase(1, 2 * T)
            barrier(dve, PH_N1)
            mlp(0)
            barrier(dve, PH_M0)
            norm_phase(2, 3 * T)
            dve.wait_ge(c1_full, 16 * 5 + 48)
            step.did(V.tensor_scalar(gainS[:, 0:4, :], gainS[:, 0:4, :], QSCALE, None, ALU.mult))
            dve.wait_ge(spilled, 16 * T)
            barrier(dve, PH_N2)
            with dve.Fori(0, NG // 2) as q:
                step.enter(q, 2 * T * 17)
                for u in range(2):
                    att_group("S", 2 * q + u + NG, 2 * q + u + G_S, 2 * q + u)
                step.leave(NG // 2)
            barrier(dve, PH_S)
            out_phase(G_O1, 4 * T, 1)
            barrier(dve, PH_O1)
            norm_phase(3, 5 * T)
            barrier(dve, PH_N3)
            mlp(1)
            barrier(dve, PH_M1)

        @block.gpsimd
        def _(pool):
            V = nc.gpsimd
            step = Steps(pool, pool_step)

            def split_lo(L, p, slot, n):
                pool.wait_ge(w_hi, 2 * L + p + 1)
                c = slice(p * n, (p + 1) * n)
                V.tensor_tensor(W_lo[:, slot, c], raw[:, p, 0:n], W_hi[:, slot, c].bitcast(f32),
                                ALU.subtract).then_inc(w_ready, 1)

            def norm_phase(m):
                for i in range(T):
                    pool.wait_ge(ss_ready, m * T + i + 1)
                    step.did(V.tensor_scalar(rstd[:, i:i + 1], ss[:, i:i + 1], 1.0 / D, EPS, ALU.mult, ALU.add))
                    step.wait()
                    V.tensor_tensor(rstd[:, i:i + 1], rstd[:, i:i + 1], neghalf[:, 0:1], ALU.pow).then_inc(rstd_ready, 1)

            def ret_group(h, slot):
                for t in range(T + 1):
                    if t >= 1:
                        n = h * T + t - 1
                        pool.wait_ge(r_var, n + 1)
                        alone(pool)
                        step.did(V.tensor_scalar(bag[:, 3:4], bag[:, 1:2], EPS, None, ALU.add))
                        step.wait()
                        V.tensor_tensor(bag[:, 2:3], bag[:, 3:4], neghalf[:, 0:1], ALU.pow).then_inc(r_rstd, 1)
                    if t in (2, 5):
                        split_lo(h + 1, t // 4, 1 - slot, 4 * W)

            def att_group(kind, qa, slot, L):
                H = 4 if kind == "D" else 5
                for t in range(T + 2):
                    if 1 <= t <= T:
                        n = qa * T + t - 1
                        pool.wait_ge(h_ss, n + 1)
                        alone(pool)
                        step.did(V.tensor_scalar(rstd[:, 0:H], ss[:, 0:H], 1.0 / HD, EPS, ALU.mult, ALU.add))
                        step.wait()
                        V.tensor_tensor(rstd[:, 0:H], rstd[:, 0:H], neghalf[:, 0:H], ALU.pow).then_inc(h_rstd, 1)
                    if t in (2, 5):
                        split_lo(L + 1, t // 4, 1 - slot, 4 * W)

            def out_phase(L):
                for j in range(1, 3):
                    for p in range(2):
                        split_lo(L + j, p, (L + j) % 2, 4 * OUTW[j])
                split_up(L + 3, (L + 3) % 2)

            def split_up(L, su):
                for p in range(2):
                    split_lo(L, p, su, 4 * FC)

            def hidden(m, c, par):
                for sh in range(2):
                    for ft in range(2):
                        n = m * 4 * NC + 4 * c + 2 * sh + ft
                        pool.wait_ge(a_hi_done, n + 1)
                        r = slice(sh * 512, (sh + 1) * 512)
                        V.tensor_tensor(a_lo[:, par, ft, r], r2[:, ft, :], a_hi[:, par, ft, r].bitcast(f32),
                                        ALU.subtract).then_inc(a_ready, 1)

            def mlp(m, LM):
                su = LM % 2
                sd = 1 - su
                split_up(LM + 1, sd)
                hidden(m, 0, 0)
                split_up(LM + 2, su)
                hidden(m, 1, 1)
                with pool.Fori(0, NC // 2 - 1) as q:
                    for u in range(2):
                        split_up(LM + 3 + 4 * q + 2 * u, su)
                        split_up(LM + 4 + 4 * q + 2 * u, sd)
                        hidden(m, 2 * q + u + 2, u)
                split_up(LM + 2 * NC - 1, sd)

            step.did(V.memset(ident[:, :], 0.0))
            step.did(V.memset(neghalf, -0.5))
            step.wait()
            step.did(V.affine_select(out=ident[:, :], in_=ident[:, :], compare_op=ALU.not_equal, fill=1.0, base=0,
                                     pattern=[[-1, P]], channel_multiplier=1))
            for n in range(HALF_R):
                step.did(V.memset(invt[:, n:n + 1], INV_R[n]))
            for n in range(HALF_D):
                step.did(V.memset(invt[:, HALF_R + n:HALF_R + n + 1], INV_D[n]))
            step.did(V.iota(df[:, 0:P], pattern=[[1, P]], base=0, channel_multiplier=-1, allow_small_or_imprecise_dtypes=True))
            step.did(V.memset(t1[:, 0:P], HD ** -0.5))
            step.wait()
            step.did(V.affine_select(out=t1[:, 0:P], in_=t1[:, 0:P], compare_op=ALU.is_ge, fill=0.0, base=0,
                                     pattern=[[1, P]], channel_multiplier=-1))
            step.did(V.tensor_scalar(df[:, 0:P], df[:, 0:P], 0.0, None, ALU.max))
            step.did(V.iota(df[:, P:P + 1], pattern=[[0, 1]], base=1, channel_multiplier=1, allow_small_or_imprecise_dtypes=True))
            step.did(V.iota(df[:, P + 1:P + 2], pattern=[[0, 1]], base=P - 1, channel_multiplier=-1, allow_small_or_imprecise_dtypes=True))
            step.did(V.memset(df[:, P + 2:P + 3], float(P)))
            step.did(V.iota(di[:, :], pattern=[[-1, T * P]], base=(T - 1) * P, channel_multiplier=1))
            assert step.n == SETUP_POOL, step.n
            barrier(pool, PH_SETUP)
            split_lo(0, 0, 0, 4 * W)
            split_lo(0, 1, 0, 4 * W)
            norm_phase(0)
            barrier(pool, PH_N0)
            with pool.Fori(0, NG // 2) as q:
                step.enter(q, 2 * T)
                for u in range(2):
                    ret_group(2 * q + u, u)
                step.leave(NG // 2)
            barrier(pool, PH_R)
            with pool.Fori(0, NG // 2) as q:
                step.enter(q, 2 * T)
                for u in range(2):
                    att_group("D", 2 * q + u, u, 2 * q + u + L_D)
                step.leave(NG // 2)
            barrier(pool, PH_D)
            out_phase(L_O0)
            barrier(pool, PH_O0)
            norm_phase(1)
            barrier(pool, PH_N1)
            mlp(0, L_M0)
            barrier(pool, PH_M0)
            step.did(V.memset(swm, 0.0))
            step.wait()
            step.did(V.affine_select(out=swm, in_=swm, compare_op=ALU.is_ge, fill=BIG, base=P, pattern=[[-1, 2 * P]],
                                     channel_multiplier=1))
            step.wait()
            step.did(V.affine_select(out=swm, in_=swm, compare_op=ALU.is_ge, fill=BIG, base=-1, pattern=[[1, 2 * P]],
                                     channel_multiplier=-1))
            split_lo(L_S, 0, L_S % 2, 4 * W)
            split_lo(L_S, 1, L_S % 2, 4 * W)
            norm_phase(2)
            barrier(pool, PH_N2)
            with pool.Fori(0, NG // 2) as q:
                step.enter(q, 2 * T)
                for u in range(2):
                    att_group("S", 2 * q + u + NG, (L_S + u) % 2, 2 * q + u + L_S)
                step.leave(NG // 2)
            barrier(pool, PH_S)
            out_phase(L_O1)
            barrier(pool, PH_O1)
            norm_phase(3)
            barrier(pool, PH_N3)
            mlp(1, L_M1)
            barrier(pool, PH_M1)


(PH_SETUP, PH_N0, PH_R, PH_D, PH_O0, PH_N1, PH_M0, PH_N2, PH_S, PH_O1, PH_N3, PH_M1) = range(1, 13)
SETUP_POOL, SETUP_SIN = 51, 12
k_xn = {0: 0, 16: 8, 24: 16, 40: 24}
INV_R = [10000.0 ** (-n * 2.0 / 64) for n in range(32)]
INV_D = [500000.0 ** (-n * 2.0 / 16) for n in range(8)]


_INS = ['x', 'positions', 'norm_mix', 'norm_mlp', 'mlp_w_up', 'mlp_w_down', 'hyb_w_in', 'hyb_w_out', 'ret_gn_gain',
        'dil_q_gain', 'dil_k_gain', 'swa_w_qkv', 'swa_b_qkv', 'swa_w_out', 'swa_q_gain', 'swa_k_gain', 'swa_sinks']


def kernel(**inputs):
    import numpy as _np
    import concourse.bacc as _bacc
    from concourse import mybir as _mybir
    from concourse.bass_utils import run_bass_kernel_spmd as _run

    nc = _bacc.Bacc("TRN2", target_bir_lowering=False, num_devices=1)
    arrays, args = {}, []
    for name in _INS:
        a = _np.ascontiguousarray(inputs[name])
        arrays[f"in_{name}"] = a
        args.append(nc.dram_tensor(f"in_{name}", a.shape, _mybir.dt.from_np(a.dtype), kind="ExternalInput").ap())
    shape = tuple(inputs['x'].shape)
    out = nc.dram_tensor("out_0", shape, _mybir.dt.float32, kind="ExternalOutput").ap()
    x_spill = nc.dram_tensor("x_spill", shape[1:], _mybir.dt.float32, kind="Internal").ap()
    hybrid_trunk(nc, *args, out, x_spill)
    r = _run(nc, [arrays], core_ids=[0])
    return r.results[0]["out_0"]
```

```python
import math

import concourse.bass as bass
from concourse import mybir
from contextlib import ExitStack


class Steps:

    def __init__(self, eng, sem):
        self.eng, self.sem, self.base, self.n = eng, sem, 0, 0

    def did(self, ins):
        ins.then_inc(self.sem, 1)
        self.n += 1

    def wait(self):
        self.eng.wait_ge(self.sem, self.base + self.n)

    def enter(self, it, per):
        self.saved, self.per = self.base + self.n, per
        self.base, self.n = self.saved + it * per, 0

    def leave(self, times):
        assert self.n == self.per, (self.n, self.per)
        self.base, self.n = self.saved + times * self.per, 0


def hybrid_trunk(nc, x_in, positions, norm_mix, norm_mlp, w_up, w_down, w_in, w_out0, gn_gain, dq_gain, dk_gain,
                 w_qkv, b_qkv, w_out1, sq_gain, sk_gain, sinks, out, x_spill):
    f32, f32r, i32 = mybir.dt.float32, mybir.dt.float32r, mybir.dt.int32
    ALU = mybir.AluOpType
    ACT = mybir.ActivationFunctionType
    AX = mybir.AxisListType

    P = 128
    S, D = x_in.shape[1], x_in.shape[2]
    T = S // P
    KD = D // P
    FF = w_up.shape[2]
    EPS = 1e-6
    HD = 64
    W = 384
    RH, RV = 4, 128
    HALF_R, HALF_D = HD // 2, HD // 8
    NG = 4
    OUTW = (384, 384, 256)
    FC = 256
    NC = FF // FC
    BIG = 1e30
    QSCALE = -(HD ** -0.5)
    GEMM_BANKS, U_BANKS, D_BANKS = 2, 4, 4
    LG = [math.log1p(-(2.0 ** (-5.0 - h))) for h in range(RH)]

    N_DR, N_O0 = 0, NG * 2 * T
    N_S = N_O0 + 3 * T
    N_O1 = N_S + NG * T
    P_DR, P_O0 = 0, NG * 8
    P_M0 = P_O0 + 12
    P_S = P_M0 + 4 * NC
    P_O1 = P_S + NG * 4
    P_M1 = P_O1 + 12
    KQ, KR = 3, 4
    F_IT = 32 * (KQ + KR)
    F_O0 = NG * F_IT
    F_M0 = F_O0 + 32 * (KQ + 2)
    F_S = F_M0 + 2 * NC * 16
    F_O1 = F_S + NG * 32 * KQ
    F_M1 = F_O1 + 32 * (KQ + 2)
    U_S, A_S = NG * 2 * T, NG * T

    ctx = ExitStack()
    with ctx:
        def sb(name, shape, dt=f32):
            return ctx.enter_context(nc.sbuf_tensor(name, shape, dt))

        def ps(name, shape):
            return ctx.enter_context(nc.psum_tensor(name, shape, f32))

        def sem(name):
            return ctx.enter_context(nc.semaphore(name))

        hT_hi = sb("hT_hi", [P, KD, S], f32r)
        hT_lo = sb("hT_lo", [P, KD, S], f32r)
        W_hi = sb("W_hi", [P, 2, KD * W], f32r)
        W_lo = sb("W_lo", [P, 2, KD * W], f32r)
        raw = sb("raw", [P, 2, 1024])
        X = sb("X", [P, T, D])
        nlm = sb("nlm", [P, T * P])
        biasS = nlm[:, 0:2 * W].rearrange("p (g n) -> p g n", g=2)
        cosR = sb("cosR", [P, T, HALF_R])
        sinR = sb("sinR", [P, T, HALF_R])
        cosD = sb("cosD", [P, T, HALF_D])
        sinD = sb("sinD", [P, T, HALF_D])
        ident = sb("ident", [P, P])
        gainD = sb("gainD", [P, 4, HD])
        c1 = sb("c1", [P, 1024])
        decay = c1[:, 0:RH * P].rearrange("p (h q) -> p h q", h=RH)
        gnB = c1[:, RH * P:2 * RH * P]
        swm = c1[:, 0:2 * P]
        gainS = c1[:, 2 * P:2 * P + 5 * HD].rearrange("p (h d) -> p h d", h=5)
        sq = sb("sq", [P, 5 * HD])
        ropeA = sb("ropeA", [P, 5 * 16])
        ropeB = sb("ropeB", [P, 5 * 16])
        rA, rB = sq[:, 0:2 * HD], sq[:, 2 * HD:4 * HD]
        st = sb("st", [P, 128])
        neghalf = st[:, 0:8]
        ss = st[:, 8:16]
        rstd = st[:, 16:24]
        xi = st[:, 24:28]
        zeta = st[:, 28:32]
        cdec = st[:, 32:36]
        negm = st[:, 36:44]
        negr = st[:, 44:52]
        den = st[:, 52:60]
        rden = st[:, 60:68]
        es = st[:, 68:76]
        nsink = st[:, 76:92]
        bst = st[:, 92:98]
        bag = st[:, 98:102]
        A0 = (nc.sbuf_base + 31) // 32 * 32
        off = [A0]

        def at(name, shape, dt=f32):
            t = nc.alloc_sbuf_tensor_at(name, shape, dt, offset=off[0])
            off[0] += 4 * int(math.prod(shape[1:]))
            assert off[0] <= nc.sbuf_usable_end, (name, off[0])
            return t

        RING = 4
        G = at("G", [P, RING, W])
        V = at("V", [P, T, 2 * HD])
        QK = at("QK", [P, 2, W])
        kT = at("kT", [P, S])
        qT = at("qT", [P, 2, 2 * P])
        Pm = at("Pm", [P, 2, 1024])
        pT = at("pT", [P, 2, 1024])
        rsT = at("rsT", [P, P])
        rR = at("rR", [HD, 2, RV])
        rsg = at("rsg", [P, 2, RV])
        re = at("re", [P, 2, RV])
        rQK = at("rQK", [P, 2, 2 * HD])
        rqT = at("rqT", [HD, 3, P])
        off[0] = A0
        a_hi, a_lo = [0, 0], [0, 0]
        a_hi[0], a_lo[0] = at("a_hi0", [P, 2, S], f32r), at("a_lo0", [P, 2, S], f32r)
        r2 = at("r2", [P, 2, 512])
        act1 = off[0]
        a_hi[1], a_lo[1] = at("a_hi1", [P, 2, S], f32r), at("a_lo1", [P, 2, S], f32r)
        trig = off[0]
        off[0] = act1
        xnA, gA, junkA = at("xnA", [P, 2, D]), at("gA", [P, D]), at("junkA", [P, D])
        off[0] = A0
        xnB, gB, junkB = at("xnB", [P, 2, D]), at("gB", [P, D]), at("junkB", [P, D])
        nbuf = [(xnA, gA, junkA), (xnA, gA, junkA), (xnB, gB, junkB), (xnA, gA, junkA)]
        off[0] = A0
        di, di4 = at("di", [P, T * P], i32), at("di4", [P, T * P], i32)
        df, t1, t2 = at("df", [P, T * P]), at("t1", [P, T * P]), at("t2", [P, T * P])
        assert off[0] <= act1
        off[0] = trig
        NA = HALF_R + HALF_D
        posi, posf = at("posi", [P, T], i32), at("posf", [P, T])
        invt, ang, nn = at("invt", [P, NA]), at("ang", [P, T, NA]), at("nn", [P, T, NA])
        tri, dq = at("tri", [P, P]), at("dq", [P, P + 3])

        gp = ps("gp", [P, 2, 512])
        sc = ps("sc", [P, 1024])
        tp = ps("tp", [P, 1024])
        o_ps = ps("o_ps", [P, 512])
        qt = ps("qt", [P, 512])
        gpf = gp[:, :, :].rearrange("p a b -> p (a b)")
        u_out = [gp[:, 0, :], gp[:, 1, :], sc[:, 0:512], sc[:, 512:1024]]
        d_out = [tp[:, 0:512], tp[:, 512:1024], o_ps[:, :], qt[:, :]]
        r_add = sc[0:HD, P:P + RV]
        r_out = sc[:, 512:512 + RV]
        nt_out = [[sc[:, :], tp[:, :]], [sc[:, :], gpf]]

        raw_full = [sem("raw_full0"), sem("raw_full1")]
        w_hi = sem("w_hi")
        w_ready = sem("w_ready")
        gains_ready = sem("gains_ready")
        x_full = [sem(f"x_full{i}") for i in range(T)]
        pos_in, const_in, sink_in, c1_in, bias_in = [
            sem(n) for n in ("pos_in", "const_in", "sink_in", "c1_in", "bias_in")]
        g_full = sem("g_full")
        spilled, stored = sem("spilled"), sem("stored")
        aside = sem("aside")
        phase = sem("phase")
        act_step, dve_step, pool_step = sem("act_step"), sem("dve_step"), sem("pool_step")
        ss_ready, rstd_ready, xn_ready, nt_done, ht_hi, ht_ready = [
            sem(n) for n in ("ss_ready", "rstd_ready", "xn_ready", "nt_done", "ht_hi", "ht_ready")]
        gemm_done, gemm_evac = sem("gemm_done"), sem("gemm_evac")
        r_exp, r_qk, r_qt, r_qtev, r_st, r_sT, r_R, r_o, r_var, r_rstd, r_x = [
            sem(n) for n in ("r_exp", "r_qk", "r_qt", "r_qtev", "r_st", "r_sT", "r_R", "r_o", "r_var",
                             "r_rstd", "r_x")]
        h_sq, h_gain, h_ss, h_rstd, qk_ready, qt_done, qkt_ready, v_ready = [
            sem(n) for n in ("h_sq", "h_gain", "h_ss", "h_rstd", "qk_ready", "qt_done", "qkt_ready", "v_ready")]
        s_done, sm_ready, p_ready, tp_done, pt_ready, pv_done, o_evac = [
            sem(n) for n in ("s_done", "sm_ready", "p_ready", "tp_done", "pt_ready", "pv_done", "o_evac")]
        u_done, u_evac, a_sq, a_hi_done, a_ready, d_done, d_evac = [
            sem(n) for n in ("u_done", "u_evac", "a_sq", "a_hi_done", "a_ready", "d_done", "d_evac")]

        def alone(eng):
            eng.sem_inc(aside, 1)

        def barrier(eng, k):
            eng.drain().then_inc(phase, 1)
            eng.wait_ge(phase, 4 * k)

        def unit(n):
            return n // (2 * T), n % (2 * T) // 2, n % 2

        def width(kind, a):
            return (a + 1) * P if kind == "D" else min(a + 1, 2) * P

        SPLIT_AT = {2: 0, 3: 1, 4: 2, 5: 3}
        PU0, PD0, PU1, PD_LAST = 0, 2, 4, 4 * NC - 2

        block = ctx.enter_context(nc.Block())

        @block.sync
        def _(sp):
            def free(first, p):
                if not (isinstance(first, int) and first + p < 2):
                    sp.wait_ge(w_ready, first + p - 1)

            def rows(w, p, n):
                return w.rearrange("(d q) n -> q d n", q=P)[:, n * p:n * (p + 1), :]

            def runs(w, parts, first):
                for p in range(4):
                    free(first, p)
                    dst = raw[:, p % 2, 0:2 * W].rearrange("q (d n) -> q d n", d=2)
                    for c, n, start in parts:
                        sp.dma_start(dst[:, :, c:c + n], rows(w, p, 2)[:, :, bass.ds(start, n)]).then_inc(raw_full[p % 2], 16)

            def load_D(g, first):
                c0 = 2 * RH * HD + 2 * RH * RV
                runs(w_in[0], [(c * 2 * HD, 2 * HD, c0 + c * 8 * HD + g * 2 * HD) for c in range(3)], first)

            def load_R(h, first):
                v = 2 * RH * HD
                runs(w_in[0], [(0, HD, h * HD), (HD, HD, RH * HD + h * HD), (2 * HD, RV, v + h * RV),
                               (2 * HD + RV, RV, v + RH * RV + h * RV)], first)

            def load_S(g, first):
                runs(w_qkv[0], [(0, 4 * HD, g * 4 * HD), (4 * HD, HD, D + g * HD), (5 * HD, HD, D + 4 * HD + g * HD)], first)

            def load_out(w, first):
                runs(w, [(c * P, P, c * P) for c in range(3)], first)
                c = OUTW[0]
                for j in (1, 2):
                    n = OUTW[j]
                    for p in range(4):
                        free(first + 4 * j, p)
                        sp.dma_start(raw[:, p % 2, 0:2 * n].rearrange("q (d n) -> q d n", d=2),
                                     rows(w, p, 2)[:, :, c:c + n]).then_inc(raw_full[p % 2], 16)
                    c += n

            def load_up(l, c, first):
                for p in range(2):
                    free(first, p)
                    sp.dma_start(raw[:, p, :].rearrange("q (d n) -> q d n", d=4),
                                 rows(w_up[l], p, 4)[:, :, bass.ds(c * FC, FC)]).then_inc(raw_full[p], 16)

            def load_down(l, c, first):
                src = w_down[l].rearrange("(c q) n -> q c n", q=P)
                for p in range(2):
                    free(first, p)
                    sp.dma_start(raw[:, p, :].rearrange("q (o n) -> q o n", o=1),
                                 src[:, bass.ds(c * 2 + p, 1), :]).then_inc(raw_full[p], 16)

            def load_mlp(l, first):
                load_up(l, 0, first + PU0)
                load_down(l, 0, first + PD0)
                load_up(l, 1, first + PU1)
                with sp.Fori(0, NC - 2) as c:
                    load_up(l, c + 2, first + 6 + 4 * c)
                    load_down(l, c + 1, first + 8 + 4 * c)
                load_down(l, NC - 1, first + PD_LAST)

            def bcast(v, n):
                return v.rearrange("(o n) -> o n", o=1).to_broadcast([P, n])

            xt = x_in[0].rearrange("(t q) d -> q t d", q=P)
            sp.dma_start(X[:, 0, :], xt[:, 0, :]).then_inc(x_full[0], 16)
            sp.dma_start(gA[:, :], bcast(norm_mix[0], D)).then_inc(g_full, 16)
            for i in range(1, T):
                sp.dma_start(X[:, i, :], xt[:, i, :]).then_inc(x_full[i], 16)
            load_D(0, P_DR)
            load_R(0, P_DR + 4)
            with sp.Fori(1, NG) as g:
                load_D(g, P_DR + 8 * g)
                load_R(g, P_DR + 8 * g + 4)
            load_out(w_out0[0], P_O0)
            load_mlp(0, P_M0)
            load_S(0, P_S)
            load_S(1, P_S + 4)
            for g in (2, 3):
                sp.wait_ge(gemm_evac, N_S + (g - 1) * T + GEMM_BANKS)
                b, dst = b_qkv[0], biasS[:, g % 2, :]
                sp.dma_start(dst[:, 0:4 * HD], bcast(b[g * 4 * HD:(g + 1) * 4 * HD], 4 * HD)).then_inc(bias_in, 16)
                for n in range(2):
                    first = D + (n * 4 + g) * HD
                    sp.dma_start(dst[:, (4 + n) * HD:(5 + n) * HD], bcast(b[first:first + HD], HD)).then_inc(bias_in, 16)
                load_S(g, P_S + 4 * g)
            load_out(w_out1[0], P_O1)
            load_mlp(1, P_M1)
            ot = out[0].rearrange("(t q) d -> q t d", q=P)
            for i in range(T):
                sp.wait_ge(d_evac, D_BANKS + 2 * 16 * NC - 16 + 2 * i + 2)
                sp.dma_start(ot[:, i, :], X[:, i, :]).then_inc(stored, 16)
            sp.wait_ge(stored, 16 * T)

        @block.tensor
        def _(pe):
            mm = nc.tensor.matmul

            def three(o, a, b, first, last):
                mm(o, a[0], b[0], start=first, stop=False)
                mm(o, a[0], b[1], start=False, stop=False)
                return mm(o, a[1], b[0], start=False, stop=last)

            def tile_T(src, i, k, side):
                b = nt_out[side][i % 2]
                if i >= 2:
                    pe.wait_ge(ht_ready, k + i - 1)
                for d in range(KD):
                    last = nc.tensor.transpose(b[:, d * P:(d + 1) * P], src[:, d * P:(d + 1) * P], ident[:, :])
                last.then_inc(nt_done, 1)

            def norm_T(m, i, k, side):
                pe.wait_ge(xn_ready, m * T + i + 1)
                tile_T(nbuf[m][0][:, i % 2, :], i, k, side)

            def gemm_steps(n, slot, i, width, piece, k):
                o = gp[:, i % 2, 0:width]
                pe.wait_ge(gemm_evac, n + 1)
                pe.wait_ge(ht_ready, k + i + 1)
                for d in range(KD):
                    if i == 0 and d % 2 == 0:
                        pe.wait_ge(w_ready, piece + d // 2 + 1)
                    c = slice(i * P, (i + 1) * P)
                    w = slice(d * width, (d + 1) * width)
                    last = three(o, (hT_hi[:, d, c], hT_lo[:, d, c]), (W_hi[:, slot, w], W_lo[:, slot, w]),
                                 d == 0, d == KD - 1)
                    if d == KD - 1:
                        last.then_inc(gemm_done, 1)
                    yield

            def nothing():
                while True:
                    yield

            def scores(kind, n, u0):
                g, a, j = unit(n)
                if j == 0:
                    pe.wait_ge(qkt_ready, (u0 + n) // 2 + 1 if isinstance(u0, int) else u0 // 2 + n // 2 + 1)
                if n >= 1:
                    pe.wait_ge(sm_ready, u0 + n)
                if kind == "D":
                    r = slice(HD * j, HD * (j + 1))
                    for c in range(0, (a + 1) * P, 512):
                        e = min(c + 512, (a + 1) * P)
                        last = mm(sc[:, c:e], qT[r, a % 2, 0:P], kT[r, c:e], start=True, stop=True)
                else:
                    k0 = max(a - 1, 0) * P
                    for e in range(2):
                        r = slice(HD * e, HD * (e + 1))
                        last = mm(sc[:, e * 512:e * 512 + (a + 1) * P - k0], qT[r, a % 2, j * P:(j + 1) * P],
                                  kT[r, k0:(a + 1) * P], start=True, stop=True)
                last.then_inc(s_done, 1)

            def blocks(kind, a):
                if kind == "D":
                    return [(c * P, c * P, c, 0) for c in range(a + 1)]
                ks = [a] if a == 0 else [a - 1, a]
                return [(e * 256 + m * P, (e * len(ks) + m) * P, c, e) for e in range(2) for m, c in enumerate(ks)]

            def trans(kind, n, u0):
                g, a, j = unit(n)
                pe.wait_ge(p_ready, u0 + n + 1)
                if n >= 1:
                    pe.wait_ge(pt_ready, u0 + n)
                for c, to, _, _ in blocks(kind, a):
                    last = nc.tensor.transpose(tp[:, to:to + P], Pm[:, j, c:c + P], ident[:, :])
                last.then_inc(tp_done, 1)

            def values(kind, n, u0):
                g, a, j = unit(n)
                pe.wait_ge(pt_ready, u0 + n + 1)
                pe.wait_ge(v_ready, (u0 // 2 if kind == "D" else A_S + (u0 - U_S) // 2) + n // 2 + 1)
                if n >= 1:
                    pe.wait_ge(o_evac, u0 + n)
                bl = blocks(kind, a)
                v0 = HD * j if kind == "D" else 0
                for m, (_, to, c, e) in enumerate(bl):
                    last = mm(o_ps[:, e * HD:(e + 1) * HD], pT[:, j, to:to + P], V[:, c, v0:v0 + HD],
                              start=(m == 0 or bl[m - 1][3] != e), stop=(m == len(bl) - 1 or bl[m + 1][3] != e))
                last.then_inc(pv_done, 1)

            def heads_T(kind, t, a0):
                pe.wait_ge(qk_ready, a0 + t + 1)
                for m in range(2 if kind == "D" else 3):
                    last = nc.tensor.transpose(qt[:, m * P:(m + 1) * P], QK[:, t % 2, m * P:(m + 1) * P], ident[:, :])
                last.then_inc(qt_done, 1)

            def ret_T(r, n):
                pe.wait_ge(r_qk, n + 1)
                alone(pe)
                q, k, qx = rQK[:, r % 2, 0:HD], rQK[:, r % 2, HD:2 * HD], QK[:, r % 2, 4 * HD:5 * HD]
                for m, src in enumerate((q, k, qx)):
                    last = nc.tensor.transpose(qt[0:HD, m * P:(m + 1) * P], src, ident[:, :])
                last.then_inc(r_qt, 1)

            def ret_scores(r, n, g):
                v = G[:, r % RING, 2 * HD:2 * HD + RV]
                if r == 0:
                    pe.wait_ge(sm_ready, (g + 1) * 2 * T)
                pe.wait_ge(r_qtev, n + 1)
                mm(sc[:, 0:P], rqT[:, 1, :], rqT[:, 0, :], start=True, stop=True)
                mm(r_add, QK[:, r % 2, 5 * HD:6 * HD], v, start=True, stop=True).then_inc(r_st, 1)

            def ret_values(r, n):
                pe.wait_ge(r_sT, n + 1)
                if r >= 1:
                    pe.wait_ge(r_x, n)
                o = r_out
                last = mm(o, rsT[:, :], G[:, r % RING, 2 * HD:2 * HD + RV], start=True, stop=(r == 0))
                if r >= 1:
                    pe.wait_ge(r_R, n)
                    last = mm(o, rqT[:, 2, :], rR[:, r % 2, :], start=False, stop=True)
                last.then_inc(r_o, 1)

            def mix_slots(kind, n0, u0, a0, slots, pieces, k, g, last_slot):
                for t in range(last_slot):
                    steps = gemm_steps(n0 + t, slots[t // T], t % T, W, pieces[t // T], k) if t < 2 * T else nothing()
                    for j in range(2):
                        n = 2 * t + j - 4
                        units = 2 * T if kind == "D" else 4 * T
                        r = t - T - 1
                        if kind == "D" and j == 1 and 0 <= r < T:
                            ret_T(r, g * T + r)
                        next(steps)
                        next(steps)
                        if 0 <= n < units:
                            scores(kind, n, u0)
                        if 0 <= n - 1 < units:
                            trans(kind, n - 1, u0)
                        if kind == "D" and j == 0 and 0 <= r - 1 < T:
                            ret_values(r - 1, g * T + r - 1)
                        next(steps)
                        if 0 <= n - 2 < units:
                            values(kind, n - 2, u0)
                        next(steps)
                        if kind == "D" and j == 1 and 0 <= r < T:
                            ret_scores(r, g * T + r, g)
                        if j == 1 and 0 <= t - 1 < units // 2:
                            heads_T(kind, t - 1, a0)

            def out_proj(n0, slots, first, k, m):
                tile_T(X[:, 0, :], 0, k, 0)
                tile_T(X[:, 1, :], 1, k, 0)
                for j, w in enumerate(OUTW):
                    for i in range(T):
                        for _ in gemm_steps(n0 + j * T + i, slots[j], i, w, first + 4 * j, k):
                            pass
                        if j == 0 and i + 2 < T:
                            tile_T(X[:, i + 2, :], i + 2, k, 0)
                        if j == 2 and i >= 2:
                            norm_T(m, i - 2, k + T, 0)

            def up(m, c, su, piece, k, middle=None):
                pe.wait_ge(w_ready, piece + 2)
                for sh in range(2):
                    pe.wait_ge(ht_ready, k + T // 2 * (sh + 1))
                    for ft in range(2):
                        o = u_out[2 * sh + ft]
                        pe.wait_ge(u_evac, m * 4 * NC + 4 * c + 2 * sh + ft + 1)
                        for d in range(KD):
                            w = slice(d * FC + ft * P, d * FC + (ft + 1) * P)
                            r = slice(sh * 512, (sh + 1) * 512)
                            last = three(o, (W_hi[:, su, w], W_lo[:, su, w]), (hT_hi[:, d, r], hT_lo[:, d, r]),
                                         d == 0, d == KD - 1)
                        last.then_inc(u_done, 1)
                    if sh == 0 and middle:
                        middle()

            def down(m, c, par, sd, piece, after=None):
                pe.wait_ge(w_ready, piece + 2)
                pe.wait_ge(a_ready, m * 4 * NC + 4 * c + 4)
                for i in range(T):
                    for nh in range(2):
                        o = d_out[(2 * i + nh) % D_BANKS]
                        pe.wait_ge(d_evac, m * 16 * NC + 16 * c + 2 * i + nh + 1)
                        for ft in range(2):
                            r = slice(i * P, (i + 1) * P)
                            w = slice(ft * D + nh * 512, ft * D + (nh + 1) * 512)
                            last = three(o, (a_hi[par][:, ft, r], a_lo[par][:, ft, r]),
                                         (W_hi[:, sd, w], W_lo[:, sd, w]), ft == 0, ft == 1)
                        last.then_inc(d_done, 1)
                    if after:
                        after(i)

            def mlp(m, first, su, k, n_out, middle, after):
                sd = 1 - su
                pe.wait_ge(gemm_evac, n_out + GEMM_BANKS)
                up(m, 0, su, first + PU0, k, middle)
                up(m, 1, su, first + PU1, k)
                down(m, 0, 0, sd, first + PD0)
                with pe.Fori(0, NC // 2 - 1) as q:
                    up(m, 2 * q + 2, su, first + 8 * q + 6, k)
                    down(m, 2 * q + 1, 1, sd, first + 8 * q + 8)
                    up(m, 2 * q + 3, su, first + 8 * q + 10, k)
                    down(m, 2 * q + 2, 0, sd, first + 8 * q + 12)
                down(m, NC - 1, 1, sd, first + PD_LAST, after)

            pe.sem_inc(gemm_evac, GEMM_BANKS)
            pe.sem_inc(u_evac, U_BANKS)
            pe.sem_inc(d_evac, D_BANKS)
            pe.wait_ge(pool_step, SETUP_ID)
            for i in range(T):
                norm_T(0, i, 0, 0)
            with pe.Fori(0, NG) as g:
                mix_slots("D", N_DR + g * 2 * T, g * 2 * T, g * T, (0, 1), (P_DR + 8 * g, P_DR + 8 * g + 4), 0, g, 2 * T + 2)
            barrier(pe, PH_DR)
            out_proj(N_O0, (0, 1, 0), P_O0, T, 1)

            def last_norms(m, k):
                norm_T(m, T - 2, k, 0)
                norm_T(m, T - 1, k, 0)

            mlp(0, P_M0, 1, 2 * T, N_O0 + 3 * T, lambda: last_norms(1, 2 * T),
                lambda i: norm_T(2, i - 2, 3 * T, 1) if i >= 2 else None)
            norm_T(2, T - 2, 3 * T, 1)
            norm_T(2, T - 1, 3 * T, 1)
            pe.wait_ge(ht_ready, 4 * T)
            with pe.Fori(0, NG // 2) as q:
                mix_slots("S", N_S + q * 2 * T, U_S + q * 4 * T, A_S + q * 2 * T, (1, 0), (P_S + 8 * q, P_S + 8 * q + 4),
                          3 * T, 0, 2 * T + 3)
            barrier(pe, PH_S)
            out_proj(N_O1, (1, 0, 1), P_O1, 4 * T, 3)
            mlp(1, P_M1, 0, 5 * T, N_O1 + 3 * T, lambda: last_norms(3, 5 * T), None)

        @block.scalar
        def _(act):
            A = nc.scalar.activation
            step = Steps(act, act_step)

            def split_hi(p, slot, width, full, rows=2):
                act.wait_ge(raw_full[p % 2], full)
                n = rows * width
                A(W_hi[:, slot, n * p:n * (p + 1)], raw[:, p % 2, 0:n], ACT.Copy).then_inc(w_hi, 1)

            def square(m, i):
                n = m * T + i
                if n >= 1:
                    act.wait_ge(ss_ready, n)
                A(nbuf[m][2][:, :], X[:, i, :], ACT.Square, accum_out=ss[:, i:i + 1]).then_inc(ss_ready, 1)

            def copy_T(i, k, side):
                act.wait_ge(nt_done, k + i + 1)
                A(hT_hi[:, :, i * P:(i + 1) * P], nt_out[side][i % 2].rearrange("p (d c) -> p d c", d=KD),
                  ACT.Copy).then_inc(ht_hi, 1)

            def mix_slots(kind, n0, u0, a0, slots, full, g, last_slot):
                units = 2 * T if kind == "D" else 4 * T
                for t in range(last_slot):
                    r = t - T - 1
                    for j in range(2):
                        if j == 0 and 1 <= t <= 2 * T and kind == "D":
                            if RING <= t - 1 < RING + T:
                                act.wait_ge(v_ready, a0 + t - RING)
                            act.wait_ge(gemm_done, n0 + t)
                            A(G[:, (t - 1) % RING, :], gp[:, (t - 1) % 2, 0:W], ACT.Copy).then_inc(gemm_evac, 1)
                            if 0 <= r:
                                act.wait_ge(gemm_evac, n0 + t + GEMM_BANKS)
                                A(re[:, r % 2, :], G[:, (t - 1) % RING, 2 * HD + RV:W], ACT.Exp, scale=-1.0).then_inc(r_exp, 1)
                        if j == 0 and 0 <= t - 1 < units // 2:
                            H = 4 if kind == "D" else 5
                            act.wait_ge(gemm_evac, n0 + t + GEMM_BANKS)
                            if not (isinstance(a0, int) and a0 + t - 1 == 0):
                                act.wait_ge(h_ss, a0 + t - 1)
                            A(sq[:, 0:H * HD], G[:, (t - 1) % RING, 0:H * HD], ACT.Square).then_inc(h_sq, 1)
                        if kind == "D" and j == 1 and 0 <= r < T:
                            act.wait_ge(r_qt, g * T + r + 1)
                            A(rqT[:, :, :].rearrange("p m c -> p (m c)"), qt[0:HD, 0:3 * P], ACT.Copy).then_inc(r_qtev, 1)
                        n = 2 * t + j - 4
                        if 0 <= n - 1 < units:
                            _, a, _ = unit(n - 1)
                            w = width(kind, a) * (1 if kind == "D" else 2)
                            act.wait_ge(tp_done, u0 + n)
                            if n - 1 >= 2:
                                act.wait_ge(pv_done, u0 + n - 2)
                            A(pT[:, (n - 1) % 2, 0:w], tp[:, 0:w], ACT.Copy).then_inc(pt_ready, 1)
                        if 0 <= n < units:
                            _, a, _ = unit(n)
                            w = width(kind, a)
                            act.wait_ge(sm_ready, u0 + n + 1)
                            if kind == "D":
                                z = n % 4
                                A(Pm[:, j, 0:w], Pm[:, j, 0:w], ACT.Exp, scale=-1.0, bias=negm[:, z:z + 1],
                                  accum_out=den[:, z:z + 1]).then_inc(p_ready, 1)
                            else:
                                z0 = 2 * (n % 4)
                                A(es[:, z0:z0 + 2], es[:, z0:z0 + 2], ACT.Exp)
                                for e in range(2):
                                    z = slice(z0 + e, z0 + e + 1)
                                    last = A(Pm[:, j, e * 256:e * 256 + w], Pm[:, j, e * 256:e * 256 + w], ACT.Exp,
                                             scale=-1.0, bias=negm[:, z], accum_out=den[:, z])
                                last.then_inc(p_ready, 1)
                        if j == 0 and t < 2 * T and t % T in SPLIT_AT:
                            p = SPLIT_AT[t % T]
                            split_hi(p, slots[1 - t // T], W, full[t // T](p))
                        if j == 1 and 0 <= t - 1 < units // 2:
                            m = 1 if kind == "D" else 2
                            act.wait_ge(qt_done, a0 + t)
                            A(qT[:, (t - 1) % 2, 0:m * P], qt[:, 0:m * P], ACT.Copy)
                            c = (t - 1) % T * P
                            A(kT[:, c:c + P], qt[:, m * P:(m + 1) * P], ACT.Copy).then_inc(qkt_ready, 1)
                if kind == "D":
                    act.wait_ge(r_x, (g + 1) * T)
                else:
                    act.wait_ge(o_evac, u0 + units)

            def gain_load(dst, v):
                act.dma_start(dst[:, :], v.rearrange("(o n) -> o n", o=1).to_broadcast([P, D])).then_inc(g_full, 16)

            def out_proj(n0, slots, F, k, m, xsrc, FM):
                for i in range(T):
                    copy_T(i, k, 0)
                    act.dma_start(X[:, i, :], xsrc[:, i, :]).then_inc(x_full[i], 16)
                for p in range(4):
                    split_hi(p, slots[1], OUTW[1], F + 32 * KQ + 16 * (p // 2 + 1))
                act.wait_ge(gemm_done, n0 + T)
                for p in range(4):
                    split_hi(p, slots[2], OUTW[2], F + 32 * (KQ + 1) + 16 * (p // 2 + 1))
                act.wait_ge(gemm_done, n0 + 2 * T)
                for p in range(2):
                    split_hi(p, slots[1], FC, FM + 16, 4)
                for i in range(T + 2):
                    if i < T:
                        act.wait_ge(gemm_evac, n0 + 2 * T + i + 1 + GEMM_BANKS)
                        square(m, i)
                    if i >= 2:
                        copy_T(i - 2, k + T, 0)

            def split_up(su, full):
                for p in range(2):
                    split_hi(p, su, FC, full, 4)

            def split_down(sd, full):
                for p in range(2):
                    split_hi(p, sd, D, full, 1)

            def hidden(m, c, par):
                for sh in range(2):
                    for ft in range(2):
                        n = m * 4 * NC + 4 * c + 2 * sh + ft
                        act.wait_ge(u_done, n + 1)
                        if not (isinstance(n, int) and n < 2):
                            act.wait_ge(a_ready, n - 1)
                        A(r2[:, ft, :], u_out[2 * sh + ft], ACT.Relu).then_inc(u_evac, 1)
                        act.wait_ge(a_sq, n + 1)
                        A(a_hi[par][:, ft, sh * 512:(sh + 1) * 512], r2[:, ft, :], ACT.Copy).then_inc(a_hi_done, 1)

            def mlp(m, su, FM, n_out):
                sd = 1 - su
                act.wait_ge(gemm_done, n_out)
                split_down(sd, FM + 32)
                hidden(m, 0, 0)
                split_up(su, FM + 48)
                hidden(m, 1, 1)
                with act.Fori(0, NC // 2 - 1) as q:
                    for u in range(2):
                        split_up(su, FM + 16 * (4 + 4 * q + 2 * u))
                        act.wait_ge(d_done, m * 16 * NC + (2 * q + u + 1) * 16)
                        split_down(sd, FM + 16 * (5 + 4 * q + 2 * u))
                        hidden(m, 2 * q + u + 2, u)
                act.wait_ge(d_done, m * 16 * NC + (NC - 1) * 16)
                split_down(sd, FM + 16 * 2 * NC)

            def bc(v, n):
                return v.rearrange("(o n) -> o n", o=1).to_broadcast([P, n])

            act.dma_start(posi[:, :], positions[0].rearrange("(t q) -> q t", q=P),
                          allow_slow_non_contiguous=True).then_inc(pos_in, 16)
            for n in range(2):
                act.dma_start(gainD[:, n, :], bc(dq_gain[0], HD)).then_inc(const_in, 16)
                act.dma_start(gainD[:, 2 + n, :], bc(dk_gain[0], HD)).then_inc(const_in, 16)
            act.dma_start(gnB, bc(gn_gain[0].rearrange("h d -> (h d)"), RH * RV)).then_inc(const_in, 16)
            act.dma_start(nsink, bc(sinks[0], 16)).then_inc(sink_in, 16)
            act.wait_ge(pool_step, SETUP_DQ)
            for h in range(RH):
                A(decay[:, h, :], dq[:, 0:P], ACT.Exp, scale=LG[h])
                A(xi[:, h:h + 1], dq[:, P:P + 1], ACT.Exp, scale=LG[h])
                A(zeta[:, h:h + 1], dq[:, P + 1:P + 2], ACT.Exp, scale=LG[h])
                last = A(cdec[:, h:h + 1], dq[:, P + 2:P + 3], ACT.Exp, scale=LG[h])
            step.did(last)
            for i in range(T + 1):
                if i < T:
                    act.wait_ge(x_full[i], 16)
                    square(0, i)
                if i >= 1:
                    copy_T(i - 1, 0, 0)
            for p in range(4):
                split_hi(p, 0, W, 16 * KQ * (p // 2 + 1))
            act.wait_ge(dve_step, SETUP_SIN)
            A(sinR[:, :, :], ang[:, :, 0:HALF_R], ACT.Sin)
            A(sinD[:, :, :], ang[:, :, HALF_R:], ACT.Sin)
            A(cosR[:, :, :], nn[:, :, 0:HALF_R], ACT.Sin)
            step.did(A(cosD[:, :, :], nn[:, :, HALF_R:], ACT.Sin))
            with act.Fori(0, NG) as g:
                mix_slots("D", N_DR + g * 2 * T, g * 2 * T, g * T, (0, 1),
                          (lambda p: g * F_IT + 32 * KQ + 16 * KR * (p // 2 + 1),
                           lambda p: (g + 1) * F_IT + 16 * KQ * (p // 2 + 1)), g, 2 * T + 2)
            barrier(act, PH_DR)
            gain_load(gA, norm_mlp[0])
            for n in range(4):
                act.dma_start(gainS[:, n, :], bc(sq_gain[0], HD)).then_inc(c1_in, 16)
            act.dma_start(gainS[:, 4, :], bc(sk_gain[0], HD)).then_inc(c1_in, 16)
            for g in range(2):
                act.dma_start(biasS[:, g, 0:4 * HD], bc(b_qkv[0, g * 4 * HD:(g + 1) * 4 * HD], 4 * HD)).then_inc(bias_in, 16)
                for n in range(2):
                    first = D + (n * 4 + g) * HD
                    act.dma_start(biasS[:, g, (4 + n) * HD:(5 + n) * HD], bc(b_qkv[0, first:first + HD], HD)).then_inc(bias_in, 16)
            xt = x_in[0].rearrange("(t q) d -> q t d", q=P)
            spill = x_spill.rearrange("(t q) d -> q t d", q=P)
            out_proj(N_O0, (0, 1, 0), F_O0, T, 1, xt, F_M0)
            mlp(0, 1, F_M0, N_O0 + 3 * T)
            gain_load(gB, norm_mix[1])
            for p in range(4):
                split_hi(p, 1, W, F_S + 16 * KQ * (p // 2 + 1))
            for i in range(T + 2):
                if i < T:
                    act.wait_ge(d_evac, D_BANKS + 16 * (NC - 1) + 2 * i + 2)
                    act.dma_start(spill[:, i, :], X[:, i, :]).then_inc(spilled, 16)
                    square(2, i)
                if i >= 2:
                    copy_T(i - 2, 3 * T, 1)
            with act.Fori(0, NG // 2) as q:
                mix_slots("S", N_S + q * 2 * T, U_S + q * 4 * T, A_S + q * 2 * T, (1, 0),
                          (lambda p: F_S + q * 64 * KQ + 32 * KQ + 16 * KQ * (p // 2 + 1),
                           lambda p: F_S + (q + 1) * 64 * KQ + 16 * KQ * (p // 2 + 1)), 0, 2 * T + 3)
            barrier(act, PH_S)
            gain_load(gA, norm_mlp[1])
            out_proj(N_O1, (1, 0, 1), F_O1, 4 * T, 3, spill, F_M1)
            mlp(1, 0, F_M1, N_O1 + 3 * T)

        @block.vector
        def _(dve):
            E = nc.vector
            step = Steps(dve, dve_step)

            def masks():
                dve.wait_ge(pool_step, SETUP_DI)
                step.did(E.tensor_scalar(di4[:, :], di[:, :], 3, None, ALU.bitwise_and))
                step.did(E.tensor_copy(df[:, :], di[:, :]))
                step.wait()
                step.did(E.tensor_scalar(di[:, :], di[:, :], 15, None, ALU.bitwise_and))
                step.did(E.tensor_scalar(t1[:, :], di4[:, :], 0.0, None, ALU.is_equal))
                step.did(E.tensor_scalar(nlm[:, :], df[:, :], 128.0, None, ALU.is_le))
                step.wait()
                step.did(E.scalar_tensor_tensor(t2[:, :], di[:, :], 0.0, nlm[:, :], ALU.is_equal, ALU.add))
                step.did(E.scalar_tensor_tensor(t1[:, :], df[:, :], 512.0, t1[:, :], ALU.is_le, ALU.mult))
                step.wait()
                step.did(E.tensor_tensor(t2[:, :], t2[:, :], t1[:, :], ALU.add))
                step.wait()
                step.did(E.scalar_tensor_tensor(t2[:, :], df[:, :], 0.0, t2[:, :], ALU.is_ge, ALU.mult))
                step.wait()
                step.did(E.tensor_scalar(nlm[:, :], t2[:, :], 0.0, BIG, ALU.is_equal, ALU.mult))
                for c in (2.0, 3.0):
                    step.wait()
                    step.did(E.tensor_scalar(t1[:, :], t2[:, :], c, -math.log(c), ALU.is_equal, ALU.mult))
                    step.wait()
                    step.did(E.tensor_tensor(nlm[:, :], nlm[:, :], t1[:, :], ALU.add))
                assert step.n == SETUP_MASK, step.n

            def angles():
                dve.wait_ge(pos_in, 16)
                step.did(E.tensor_copy(posf[:, :], posi[:, :]))
                dve.wait_ge(pool_step, SETUP_POOL)
                step.wait()
                n3 = [P, T, NA]
                step.did(E.tensor_tensor(ang[:, :, :], posf[:, :].rearrange("p (t o) -> p t o", o=1).to_broadcast(n3),
                                         invt[:, :].rearrange("p (o n) -> p o n", o=1).to_broadcast(n3), ALU.mult))
                step.wait()
                magic = 1.5 * 2.0 ** 23
                step.did(E.tensor_scalar(nn[:, :, :], ang[:, :, :], 1.0 / (2 * math.pi), magic, ALU.mult, ALU.add))
                step.wait()
                step.did(E.tensor_scalar(nn[:, :, :], nn[:, :, :], magic, None, ALU.subtract))
                left = 2 * math.pi
                for bits in (5, 13, 21, None):
                    part = left if bits is None else math.floor(left * 2.0 ** bits) / 2.0 ** bits
                    left -= part
                    step.wait()
                    step.did(E.scalar_tensor_tensor(ang[:, :, :], nn[:, :, :], -part, ang[:, :, :], ALU.mult, ALU.add))
                step.wait()
                lim = 3.1415925
                step.did(E.tensor_scalar(ang[:, :, :], ang[:, :, :], lim, -lim, ALU.min, ALU.max))
                step.wait()
                step.did(E.tensor_scalar(nn[:, :, :], ang[:, :, :], -1.0, None, ALU.mult))
                step.wait()
                step.did(E.tensor_tensor(nn[:, :, :], nn[:, :, :], ang[:, :, :], ALU.max))
                step.wait()
                step.did(E.tensor_scalar(nn[:, :, :], nn[:, :, :], -1.0, math.pi / 2, ALU.mult, ALU.add))
                assert step.n == SETUP_SIN, step.n
                dve.wait_ge(const_in, 16 * 5)
                E.tensor_scalar(gainD[:, 0:2, :], gainD[:, 0:2, :], QSCALE, None, ALU.mult).then_inc(gains_ready, 1)
                dve.wait_ge(act_step, 1)
                step.did(E.tensor_tensor(decay, decay, tri[:, :].rearrange("p (o q) -> p o q", o=1).to_broadcast([P, RH, P]),
                                         ALU.mult))
                step.did(E.tensor_scalar(zeta, zeta, HD ** -0.5, None, ALU.mult))
                step.wait()
                dve.wait_ge(act_step, 2)

            def lo_T(i, k, side):
                dve.wait_ge(ht_hi, k + i + 1)
                c = slice(i * P, (i + 1) * P)
                E.tensor_tensor(hT_lo[:, :, c], nt_out[side][i % 2].rearrange("p (d c) -> p d c", d=KD),
                                hT_hi[:, :, c].bitcast(f32), ALU.subtract).then_inc(ht_ready, 1)

            def normed(m, i, k):
                xn, gain, _ = nbuf[m]
                if i == 0:
                    dve.wait_ge(g_full, 16 * (m + 1))
                dve.wait_ge(rstd_ready, m * T + i + 1)
                if i >= 2:
                    dve.wait_ge(nt_done, k + i - 1)
                E.scalar_tensor_tensor(xn[:, i % 2, :], X[:, i, :], rstd[:, i:i + 1], gain[:, :], ALU.mult,
                                       ALU.mult).then_inc(xn_ready, 1)

            def ret_rope(h, r, n, evac):
                dve.wait_ge(gemm_evac, evac)
                if r >= 2:
                    dve.wait_ge(r_x, n - 1)
                g = G[:, r % RING, :]
                x = g[:, 0:2 * HD].rearrange("p (m s d) -> p m s d", m=2, s=2)
                A4 = rA.rearrange("p (m s d) -> p m s d", m=2, s=2)
                B4 = rB.rearrange("p (m s d) -> p m s d", m=2, s=2)
                cc = cosR[:, r, :].rearrange("p (m s d) -> p m s d", m=1, s=1).to_broadcast([P, 2, 2, HALF_R])
                sn = sinR[:, r, :].rearrange("p (m d) -> p m d", m=1).to_broadcast([P, 2, HALF_R])
                step.wait()
                step.did(E.tensor_tensor(A4, x, cc, ALU.mult))
                step.did(E.scalar_tensor_tensor(B4[:, :, 0, :], x[:, :, 1, :], -1.0, sn, ALU.mult, ALU.mult))
                step.did(E.tensor_tensor(B4[:, :, 1, :], x[:, :, 0, :], sn, ALU.mult))
                step.wait()
                q = rQK[:, r % 2, :]
                step.did(E.tensor_tensor(q, rA, rB, ALU.add))
                step.wait()
                step.did(E.tensor_scalar(QK[:, r % 2, 4 * HD:5 * HD], q[:, 0:HD], xi[:, bass.ds(h, 1)], None, ALU.mult))
                E.tensor_scalar(QK[:, r % 2, 5 * HD:6 * HD], q[:, HD:2 * HD], zeta[:, bass.ds(h, 1)], None,
                                ALU.mult).then_inc(r_qk, 1)
                dve.wait_ge(r_exp, n + 1)
                e, o = re[:, r % 2, :], rsg[:, r % 2, :]
                step.did(E.tensor_scalar(e, e, 1.0, None, ALU.add))
                step.did(E.tensor_tensor(o, g[:, 2 * HD + RV:W], gnB[:, bass.ds(h * RV, RV)], ALU.mult))
                step.wait()
                step.did(E.reciprocal(e, e))
                step.wait()
                step.did(E.tensor_tensor(o, o, e, ALU.mult))

            def ret_state(h, r, n):
                dve.wait_ge(r_st, n + 1)
                E.tensor_tensor(rsT[:, :], sc[:, 0:P], decay[:, bass.ds(h, 1), :].rearrange("p o q -> p (o q)"),
                                ALU.mult).then_inc(r_sT, 1)
                new = rR[:, (r + 1) % 2, :]
                if r == 0:
                    E.tensor_copy(new, r_add).then_inc(r_R, 1)
                else:
                    dve.wait_ge(r_R, n)
                    E.scalar_tensor_tensor(new, rR[:, r % 2, :], cdec[0:HD, bass.ds(h, 1)], r_add,
                                           ALU.mult, ALU.add).then_inc(r_R, 1)

            def ret_out(h, r, n):
                dve.wait_ge(r_o, n + 1)
                step.did(E.bn_stats(bst, r_out))
                step.wait()
                alone(dve)
                E.bn_aggr(bag[:, 0:2], bst).then_inc(r_var, 1)
                dve.wait_ge(r_rstd, n + 1)
                step.did(E.tensor_scalar(rA, r_out, bag[:, 0:1], bag[:, 2:3], ALU.subtract, ALU.mult))
                step.wait()
                E.tensor_tensor(X[:, r, bass.ds(h * RV, RV)], rA, rsg[:, r % 2, :], ALU.mult).then_inc(r_x, 1)

            def sums(kind, t, a0):
                H = 4 if kind == "D" else 5
                dve.wait_ge(h_sq, a0 + t + 1)
                alone(dve)
                E.tensor_reduce(ss[:, 0:H], sq[:, 0:H * HD].rearrange("p (h d) -> p h d", h=H), AX.X, ALU.add).then_inc(h_ss, 1)

            def prep(kind, t, a0):
                H = 4 if kind == "D" else 5
                q = QK[:, t % 2, 0:H * HD].rearrange("p (h d) -> p h d", h=H)
                dve.wait_ge(h_gain, a0 + t + 1)
                dve.wait_ge(h_rstd, a0 + t + 1)
                rb = rstd[:, 0:H].rearrange("p (h o) -> p h o", o=1).to_broadcast([P, H, HD])
                step.did(E.tensor_tensor(q, q, rb, ALU.mult))
                A3 = ropeA[:, 0:H * 16].rearrange("p (h s d) -> p h s d", h=H, s=2)
                B3 = ropeB[:, 0:H * 16].rearrange("p (h s d) -> p h s d", h=H, s=2)
                q4 = q[:, :, 0:2 * HALF_D].rearrange("p h (s d) -> p h s d", s=2)
                cc = cosD[:, t % T, :].rearrange("p (m s d) -> p m s d", m=1, s=1).to_broadcast([P, H, 2, HALF_D])
                sn = sinD[:, t % T, :].rearrange("p (m d) -> p m d", m=1).to_broadcast([P, H, HALF_D])
                step.wait()
                step.did(E.tensor_tensor(A3, q4, cc, ALU.mult))
                step.did(E.scalar_tensor_tensor(B3[:, :, 0, :], q4[:, :, 1, :], -1.0, sn, ALU.mult, ALU.mult))
                step.did(E.tensor_tensor(B3[:, :, 1, :], q4[:, :, 0, :], sn, ALU.mult))
                step.wait()
                if kind == "D":
                    E.tensor_tensor(q4, A3, B3, ALU.add).then_inc(qk_ready, 1)
                else:
                    step.did(E.tensor_tensor(q4, A3, B3, ALU.add))
                    step.wait()
                    E.tensor_copy(QK[:, t % 2, 5 * HD:6 * HD], QK[:, t % 2, 4 * HD:5 * HD]).then_inc(qk_ready, 1)

            def maxima(kind, n, u0, g):
                gg, a, j = unit(n)
                if n >= 2:
                    dve.wait_ge(tp_done, u0 + n - 1)
                dve.wait_ge(s_done, u0 + n + 1)
                alone(dve)
                w = width(kind, a)
                if kind == "D":
                    z = n % 4
                    E.tensor_tensor_reduce(out=Pm[:, j, 0:w], in0=sc[:, 0:w], in1=nlm[:, (T - 1 - a) * P:T * P], scale=1.0,
                                           scalar=3e38, op0=ALU.add, op1=ALU.min, accum_out=negm[:, z:z + 1]).then_inc(sm_ready, 1)
                    return
                z = 2 * (n % 4)
                for e in range(2):
                    step.did(E.tensor_tensor_reduce(out=Pm[:, j, e * 256:e * 256 + w], in0=sc[:, e * 512:e * 512 + w],
                                                    in1=swm[:, 256 - w:256], scale=1.0, scalar=3e38, op0=ALU.add,
                                                    op1=ALU.min, accum_out=negr[:, z + e:z + e + 1]))
                step.wait()
                sk = nsink[:, bass.ds((g + gg) * 4 + 2 * j, 2)]
                step.did(E.tensor_tensor(negm[:, z:z + 2], negr[:, z:z + 2], sk, ALU.min))
                step.wait()
                E.tensor_tensor(es[:, z:z + 2], negm[:, z:z + 2], sk, ALU.subtract).then_inc(sm_ready, 1)

            def outputs(kind, n, u0, g):
                gg, a, j = unit(n)
                if kind == "D":
                    z = n % 4
                    dve.wait_ge(pv_done, u0 + n + 1)
                    step.did(E.reciprocal(rden[:, z:z + 1], den[:, z:z + 1]))
                    step.wait()
                    E.tensor_scalar(X[:, a, bass.ds(g * 2 * HD + D // 2 + j * HD, HD)], o_ps[:, 0:HD],
                                    rden[:, z:z + 1], None, ALU.mult).then_inc(o_evac, 1)
                    return
                z = slice(2 * (n % 4), 2 * (n % 4) + 2)
                dve.wait_ge(pv_done, u0 + n + 1)
                step.did(E.tensor_tensor(den[:, z], den[:, z], es[:, z], ALU.add))
                step.wait()
                step.did(E.reciprocal(rden[:, z], den[:, z]))
                step.wait()
                E.tensor_tensor(X[:, a, bass.ds((g + gg) * 4 * HD + 2 * j * HD, 2 * HD)].rearrange("p (e d) -> p e d", e=2),
                                o_ps[:, 0:2 * HD].rearrange("p (e d) -> p e d", e=2),
                                rden[:, z].rearrange("p (e o) -> p e o", o=1).to_broadcast([P, 2, HD]), ALU.mult).then_inc(o_evac, 1)

            def mix_slots(kind, n0, u0, a0, g, last_slot):
                units = 2 * T if kind == "D" else 4 * T
                for t in range(last_slot):
                    r = t - T - 1
                    for j in range(2):
                        n = 2 * t + j - 4
                        if kind == "S" and j == 0 and 1 <= t <= 2 * T:
                            if t - 1 >= RING:
                                dve.wait_ge(v_ready, a0 + t - RING)
                            if (t - 1) % T == 0:
                                dve.wait_ge(bias_in, 48 * (g + t // T + 1))
                            dve.wait_ge(gemm_done, n0 + t)
                            E.tensor_tensor(G[:, (t - 1) % RING, :], gp[:, (t - 1) % 2, 0:W], biasS[:, (t - 1) // T, :],
                                            ALU.add).then_inc(gemm_evac, 1)
                        if 0 <= n - 3 < units:
                            outputs(kind, n - 3, u0, g)
                        if j == 0 and 0 <= t - 1 < units // 2:
                            sums(kind, t - 1, a0)
                        if 0 <= n < units:
                            maxima(kind, n, u0, g)
                        if j == 0 and 0 <= t - 1 < units // 2:
                            prep(kind, t - 1, a0)
                        if kind == "D":
                            if j == 0 and 0 <= r < T:
                                ret_rope(g, r, g * T + r, n0 + t + GEMM_BANKS)
                            if j == 0 and 0 <= r - 1 < T:
                                ret_out(g, r - 1, g * T + r - 1)
                            if j == 1 and 0 <= r < T:
                                ret_state(g, r, g * T + r)

            def out_proj(n0, k, m, full):
                lo_T(0, k, 0)
                lo_T(1, k, 0)
                c = 0
                for j, w in enumerate(OUTW):
                    for i in range(T + (2 if j == 2 else 0)):
                        if i < T:
                            if j == 0:
                                dve.wait_ge(x_full[i], full)
                            dve.wait_ge(gemm_done, n0 + j * T + i + 1)
                            E.tensor_tensor(X[:, i, c:c + w], gp[:, i % 2, 0:w], X[:, i, c:c + w], ALU.add).then_inc(gemm_evac, 1)
                        if j == 0 and i + 2 < T:
                            lo_T(i + 2, k, 0)
                        if j == 2 and 1 <= i <= T:
                            normed(m, i - 1, k + T)
                        if j == 2 and i >= 2:
                            lo_T(i - 2, k + T, 0)
                    c += w

            def square(m, c):
                for sh in range(2):
                    for ft in range(2):
                        n = m * 4 * NC + 4 * c + 2 * sh + ft
                        dve.wait_ge(u_evac, n + 1 + U_BANKS)
                        E.tensor_tensor(r2[:, ft, :], r2[:, ft, :], r2[:, ft, :], ALU.mult).then_inc(a_sq, 1)

            def add_down(m, c, i):
                for nh in range(2):
                    n = m * 16 * NC + 16 * c + 2 * i + nh
                    dve.wait_ge(d_done, n + 1)
                    x = X[:, i, nh * 512:(nh + 1) * 512]
                    E.tensor_tensor(x, d_out[(2 * i + nh) % D_BANKS], x, ALU.add).then_inc(d_evac, 1)

            def mlp(m):
                square(m, 0)
                square(m, 1)
                with dve.Fori(0, NC - 2) as c:
                    for i in range(T):
                        add_down(m, c, i)
                    square(m, c + 2)
                for i in range(T):
                    add_down(m, NC - 2, i)

            masks()
            for i in range(T + 1):
                if i < T:
                    normed(0, i, 0)
                if i >= 1:
                    lo_T(i - 1, 0, 0)
            angles()
            with dve.Fori(0, NG) as g:
                step.enter(g, T * 4 + 2 * T + T * 11)
                mix_slots("D", N_DR + g * 2 * T, g * 2 * T, g * T, g, 2 * T + 2)
                step.leave(NG)
            barrier(dve, PH_DR)
            out_proj(N_O0, T, 1, 32)
            mlp(0)
            for i in range(T + 2):
                if i < T:
                    add_down(0, NC - 1, i)
                if 1 <= i <= T:
                    normed(2, i - 1, 3 * T)
                if i >= 2:
                    lo_T(i - 2, 3 * T, 1)
            dve.wait_ge(c1_in, 16 * 5)
            E.tensor_scalar(gainS[:, 0:4, :], gainS[:, 0:4, :], QSCALE, None, ALU.mult).then_inc(gains_ready, 1)
            dve.wait_ge(sink_in, 16)
            step.did(E.tensor_scalar(nsink, nsink, -1.0, None, ALU.mult))
            step.wait()
            dve.wait_ge(pool_step, SETUP_POOL + NG * 2 * T + 3)
            dve.wait_ge(spilled, 16 * T)
            with dve.Fori(0, NG // 2) as q:
                step.enter(q, 2 * T * 5 + 4 * T * 5)
                mix_slots("S", N_S + q * 2 * T, U_S + q * 4 * T, A_S + q * 2 * T, 2 * q, 2 * T + 4)
                step.leave(NG // 2)
            barrier(dve, PH_S)
            out_proj(N_O1, 4 * T, 3, 48)
            mlp(1)
            for i in range(T):
                add_down(1, NC - 1, i)

        @block.gpsimd
        def _(pool):
            E = nc.gpsimd
            step = Steps(pool, pool_step)

            def split_lo(piece, p, slot, n):
                pool.wait_ge(w_hi, piece + p + 1)
                c = slice(p * n, (p + 1) * n)
                E.tensor_tensor(W_lo[:, slot, c], raw[:, p % 2, 0:n], W_hi[:, slot, c].bitcast(f32),
                                ALU.subtract).then_inc(w_ready, 1)

            def norm_rstd(m, i):
                pool.wait_ge(ss_ready, m * T + i + 1)
                step.did(E.tensor_scalar(rstd[:, i:i + 1], ss[:, i:i + 1], 1.0 / D, EPS, ALU.mult, ALU.add))
                step.wait()
                E.tensor_tensor(rstd[:, i:i + 1], rstd[:, i:i + 1], neghalf[:, 0:1], ALU.pow).then_inc(rstd_ready, 1)

            def mix_slots(kind, n0, u0, a0, slots, pieces, g, last_slot):
                H = 4 if kind == "D" else 5
                units = 2 * T if kind == "D" else 4 * T
                gain = gainD[:, :, :] if kind == "D" else gainS
                for t in range(last_slot):
                    r = t - T - 1
                    if 0 <= t - 1 < units // 2:
                        pool.wait_ge(gemm_evac, n0 + t + GEMM_BANKS)
                        if t - 1 >= 2:
                            pool.wait_ge(qt_done, a0 + t - 2)
                        E.tensor_tensor(QK[:, (t - 1) % 2, 0:H * HD].rearrange("p (h d) -> p h d", h=H),
                                        G[:, (t - 1) % RING, 0:H * HD].rearrange("p (h d) -> p h d", h=H),
                                        gain, ALU.mult).then_inc(h_gain, 1)
                    if 0 <= t - 3 < units // 2:
                        if kind == "D":
                            E.tensor_copy(V[:, t - 3, :], G[:, (t - 3) % RING, 4 * HD:6 * HD]).then_inc(v_ready, 1)
                        else:
                            E.tensor_copy(V[:, (t - 3) % T, 0:HD], G[:, (t - 3) % RING, 5 * HD:6 * HD]).then_inc(v_ready, 1)
                    if 0 <= t - 1 < units // 2:
                        pool.wait_ge(h_ss, a0 + t)
                        alone(pool)
                        step.did(E.tensor_scalar(rstd[:, 0:H], ss[:, 0:H], 1.0 / HD, EPS, ALU.mult, ALU.add))
                        step.wait()
                        E.tensor_tensor(rstd[:, 0:H], rstd[:, 0:H], neghalf[:, 0:H], ALU.pow).then_inc(h_rstd, 1)
                    if kind == "D" and 0 <= r - 1 < T:
                        pool.wait_ge(r_var, g * T + r)
                        alone(pool)
                        step.did(E.tensor_scalar(bag[:, 3:4], bag[:, 1:2], EPS, None, ALU.add))
                        step.wait()
                        E.tensor_tensor(bag[:, 2:3], bag[:, 3:4], neghalf[:, 0:1], ALU.pow).then_inc(r_rstd, 1)
                    if t < 2 * T and t % T in SPLIT_AT:
                        split_lo(pieces[t // T], SPLIT_AT[t % T], slots[1 - t // T], 2 * W)

            def out_proj(first, slots, m, PM):
                for j in (1, 2):
                    for p in range(4):
                        split_lo(first + 4 * j, p, slots[j], 2 * OUTW[j])
                split_two(PM + PU0, slots[1])
                for i in range(T):
                    norm_rstd(m, i)

            def split_two(piece, slot):
                for p in range(2):
                    split_lo(piece, p, slot, 1024)

            def hidden(m, c, par):
                for sh in range(2):
                    for ft in range(2):
                        n = m * 4 * NC + 4 * c + 2 * sh + ft
                        pool.wait_ge(a_hi_done, n + 1)
                        r = slice(sh * 512, (sh + 1) * 512)
                        E.tensor_tensor(a_lo[par][:, ft, r], r2[:, ft, :], a_hi[par][:, ft, r].bitcast(f32),
                                        ALU.subtract).then_inc(a_ready, 1)

            def mlp(m, first, su):
                sd = 1 - su
                split_two(first + PD0, sd)
                hidden(m, 0, 0)
                split_two(first + PU1, su)
                hidden(m, 1, 1)
                with pool.Fori(0, NC // 2 - 1) as q:
                    for u in range(2):
                        split_two(first + 6 + 8 * q + 4 * u, su)
                        split_two(first + 8 + 8 * q + 4 * u, sd)
                        hidden(m, 2 * q + u + 2, u)
                split_two(first + PD_LAST, sd)

            step.did(E.iota(di[:, :], pattern=[[-1, T * P]], base=(T - 1) * P, channel_multiplier=1))
            step.did(E.memset(ident[:, :], 0.0))
            step.did(E.memset(neghalf, -0.5))
            step.did(E.iota(dq[:, 0:P], pattern=[[1, P]], base=0, channel_multiplier=-1, allow_small_or_imprecise_dtypes=True))
            step.did(E.memset(tri[:, :], HD ** -0.5))
            step.did(E.iota(dq[:, P:P + 1], pattern=[[0, 1]], base=1, channel_multiplier=1, allow_small_or_imprecise_dtypes=True))
            step.did(E.iota(dq[:, P + 1:P + 2], pattern=[[0, 1]], base=P - 1, channel_multiplier=-1, allow_small_or_imprecise_dtypes=True))
            step.did(E.memset(dq[:, P + 2:P + 3], float(P)))
            step.wait()
            step.did(E.affine_select(out=ident[:, :], in_=ident[:, :], compare_op=ALU.not_equal, fill=1.0, base=0,
                                     pattern=[[-1, P]], channel_multiplier=1))
            assert step.n == SETUP_ID, step.n
            step.did(E.tensor_scalar(dq[:, 0:P], dq[:, 0:P], 0.0, None, ALU.max))
            assert step.n == SETUP_DQ, step.n
            step.did(E.affine_select(out=tri[:, :], in_=tri[:, :], compare_op=ALU.is_ge, fill=0.0, base=0,
                                     pattern=[[1, P]], channel_multiplier=-1))
            for n in range(HALF_R):
                step.did(E.memset(invt[:, n:n + 1], INV_R[n]))
            for n in range(HALF_D):
                step.did(E.memset(invt[:, HALF_R + n:HALF_R + n + 1], INV_D[n]))
            assert step.n == SETUP_POOL - T, step.n
            for i in range(T):
                norm_rstd(0, i)
            for p in range(4):
                split_lo(P_DR, p, 0, 2 * W)
            pool.wait_ge(const_in, 16 * 5)
            pool.wait_ge(gains_ready, 1)
            with pool.Fori(0, NG) as g:
                step.enter(g, 2 * T)
                mix_slots("D", N_DR + g * 2 * T, g * 2 * T, g * T, (0, 1), (P_DR + 8 * g + 4, P_DR + 8 * g + 8), g, 2 * T + 2)
                step.leave(NG)
            barrier(pool, PH_DR)
            step.did(E.memset(swm, 0.0))
            step.wait()
            step.did(E.affine_select(out=swm, in_=swm, compare_op=ALU.is_ge, fill=BIG, base=P, pattern=[[-1, 2 * P]],
                                     channel_multiplier=1))
            step.wait()
            step.did(E.affine_select(out=swm, in_=swm, compare_op=ALU.is_ge, fill=BIG, base=-1, pattern=[[1, 2 * P]],
                                     channel_multiplier=-1))
            out_proj(P_O0, (0, 1, 0), 1, P_M0)
            mlp(0, P_M0, 1)
            for p in range(4):
                split_lo(P_S, p, 1, 2 * W)
            for i in range(T):
                norm_rstd(2, i)
            pool.wait_ge(c1_in, 16 * 5)
            pool.wait_ge(gains_ready, 2)
            with pool.Fori(0, NG // 2) as q:
                step.enter(q, 2 * T)
                mix_slots("S", N_S + q * 2 * T, U_S + q * 4 * T, A_S + q * 2 * T, (1, 0), (P_S + 8 * q + 4, P_S + 8 * q + 8), 0, 2 * T + 3)
                step.leave(NG // 2)
            barrier(pool, PH_S)
            out_proj(P_O1, (1, 0, 1), 3, P_M1)
            mlp(1, P_M1, 0)


PH_DR, PH_S = 1, 2
SETUP_DI, SETUP_ID, SETUP_DQ, SETUP_POOL = 1, 9, 10, 59
SETUP_MASK, SETUP_SIN = 14, 26
INV_R = [10000.0 ** (-n * 2.0 / 64) for n in range(32)]
INV_D = [500000.0 ** (-n * 2.0 / 16) for n in range(8)]


_INS = ['x', 'positions', 'norm_mix', 'norm_mlp', 'mlp_w_up', 'mlp_w_down', 'hyb_w_in', 'hyb_w_out', 'ret_gn_gain',
        'dil_q_gain', 'dil_k_gain', 'swa_w_qkv', 'swa_b_qkv', 'swa_w_out', 'swa_q_gain', 'swa_k_gain', 'swa_sinks']


def kernel(**inputs):
    import numpy as _np
    import concourse.bacc as _bacc
    from concourse import mybir as _mybir
    from concourse.bass_utils import run_bass_kernel_spmd as _run

    nc = _bacc.Bacc("TRN2", target_bir_lowering=False, num_devices=1)
    arrays, args = {}, []
    for name in _INS:
        a = _np.ascontiguousarray(inputs[name])
        arrays[f"in_{name}"] = a
        args.append(nc.dram_tensor(f"in_{name}", a.shape, _mybir.dt.from_np(a.dtype), kind="ExternalInput").ap())
    shape = tuple(inputs['x'].shape)
    out = nc.dram_tensor("out_0", shape, _mybir.dt.float32, kind="ExternalOutput").ap()
    x_spill = nc.dram_tensor("x_spill", shape[1:], _mybir.dt.float32, kind="Internal").ap()
    hybrid_trunk(nc, *args, out, x_spill)
    r = _run(nc, [arrays], core_ids=[0])
    return r.results[0]["out_0"]
```
